# Optimizing a Trainium2 kernel written in Bass

```python
import math
import jax, jax.numpy as jnp
from jax import lax
import numpy as np

D_MODEL = 1024
BATCH = 1
SEQ = 256
DEPTH = 2

HEAD_DIM = 64
ATT_WIDTH = D_MODEL // 2
ATT_HEADS = ATT_WIDTH // HEAD_DIM
SG_WIDTH = D_MODEL // 4
SG_GROUPS = 4
SG_GROUP_DIM = SG_WIDTH // SG_GROUPS
CONV_WIDTH = D_MODEL // 4
MIX_WIDTH = ATT_WIDTH + SG_WIDTH + CONV_WIDTH

Q_OFF = 0
K_OFF = Q_OFF + ATT_WIDTH
V_OFF = K_OFF + ATT_WIDTH
SGU_OFF = V_OFF + ATT_WIDTH
SGV_OFF = SGU_OFF + SG_WIDTH
CA_OFF = SGV_OFF + SG_WIDTH
CG_OFF = CA_OFF + CONV_WIDTH
IN_COLS = CG_OFF + CONV_WIDTH

MOBA_BLOCK = 256
MOBA_TOPK = 3
Q_CHUNK = 128
SG_CHUNK = 128
CONV_TAPS = 31
ROPE_THETA = 10000.0
N_EXPERTS = 16
N_EXPERT_GROUPS = 4
EXPERTS_PER_GROUP = N_EXPERTS // N_EXPERT_GROUPS
TOP_K = 2
D_EXPERT = D_MODEL // 2
LN_EPS = 1e-5
NEG = -1e30
DEEPNORM_ALPHA = (2.0 * DEPTH) ** 0.25
DEEPNORM_BETA = (8.0 * DEPTH) ** -0.25

kernel_name = "hymba_moba_gmlp_conformer_grouped_moe"

def layer_norm(x, g, b):
    xf = x.astype(jnp.float32)
    mu = jnp.mean(xf, axis=-1, keepdims=True)
    var = jnp.mean(jnp.square(xf - mu), axis=-1, keepdims=True)
    return ((xf - mu) * lax.rsqrt(var + LN_EPS) * g + b).astype(x.dtype)

def rotary(x):
    s = x.shape[1]
    half = HEAD_DIM // 2
    inv_freq = ROPE_THETA ** (-jnp.arange(half, dtype=jnp.float32) / half)
    ang = jnp.arange(s, dtype=jnp.float32)[:, None] * inv_freq[None, :]
    cos = jnp.cos(ang)[None, :, None, :]
    sin = jnp.sin(ang)[None, :, None, :]
    xf = x.astype(jnp.float32)
    x1, x2 = xf[..., :half], xf[..., half:]
    return jnp.concatenate([x1 * cos - x2 * sin, x2 * cos + x1 * sin], axis=-1).astype(x.dtype)

def moba_attention(q, k, v):
    b, s, h, dh = q.shape
    bh = b * h
    nb = -(-s // MOBA_BLOCK)
    pad = nb * MOBA_BLOCK - s
    k_top = min(MOBA_TOPK, nb)
    to_g = lambda t: t.transpose(0, 2, 1, 3).reshape(bh, s, dh)
    qg, kg, vg = to_g(q), to_g(k), to_g(v)
    kb = jnp.pad(kg, ((0, 0), (0, pad), (0, 0))).reshape(bh, nb, MOBA_BLOCK, dh)
    vb = jnp.pad(vg, ((0, 0), (0, pad), (0, 0))).reshape(bh, nb, MOBA_BLOCK, dh)
    kmean = jnp.mean(kb.astype(jnp.float32), axis=2)
    nc = s // Q_CHUNK
    qc = qg.reshape(bh, nc, Q_CHUNK, dh).transpose(1, 0, 2, 3)
    scale = HEAD_DIM ** -0.5
    g_idx = jnp.arange(bh)[:, None, None]
    blk_ids = jnp.arange(nb)
    sel_rank = jnp.arange(k_top)

    def one_chunk(args):
        qi, c = args
        q_pos = c * Q_CHUNK + jnp.arange(Q_CHUNK)
        own = (c * Q_CHUNK) // MOBA_BLOCK
        gate = jnp.einsum('gqd,gnd->gqn', qi.astype(jnp.float32), kmean)
        gate = jnp.where((blk_ids < own)[None, None, :], gate, NEG)
        _, sel = lax.top_k(gate, k_top)
        sel_ok = sel_rank < own
        k_sel = kb[g_idx, sel]
        v_sel = vb[g_idx, sel]
        s_sel = jnp.einsum('gqd,gqnkd->gqnk', qi, k_sel).astype(jnp.float32) * scale
        s_sel = jnp.where(sel_ok[None, None, :, None], s_sel, NEG).reshape(bh, Q_CHUNK, k_top * MOBA_BLOCK)
        k_own = lax.dynamic_index_in_dim(kb, own, axis=1, keepdims=False)
        v_own = lax.dynamic_index_in_dim(vb, own, axis=1, keepdims=False)
        s_own = jnp.einsum('gqd,gkd->gqk', qi, k_own).astype(jnp.float32) * scale
        k_pos = own * MOBA_BLOCK + jnp.arange(MOBA_BLOCK)
        s_own = jnp.where((k_pos[None, :] <= q_pos[:, None])[None], s_own, NEG)
        p = jax.nn.softmax(jnp.concatenate([s_sel, s_own], axis=-1), axis=-1)
        p_sel = p[..., :k_top * MOBA_BLOCK].reshape(bh, Q_CHUNK, k_top, MOBA_BLOCK).astype(v.dtype)
        p_own = p[..., k_top * MOBA_BLOCK:].astype(v.dtype)
        return (jnp.einsum('gqnk,gqnkd->gqd', p_sel, v_sel)
                + jnp.einsum('gqk,gkd->gqd', p_own, v_own))

    out = lax.map(one_chunk, (qc, jnp.arange(nc)))
    out = out.transpose(1, 0, 2, 3).reshape(b, h, s, dh).transpose(0, 2, 1, 3)
    return out.reshape(b, s, h * dh)

def spatial_gating(u, v, ln_g, ln_b, w_s, b_s):
    b, s, _ = v.shape
    v = layer_norm(v, ln_g, ln_b)
    vc = v.reshape(b, s // SG_CHUNK, SG_CHUNK, SG_GROUPS, SG_GROUP_DIM)
    causal = jnp.tril(jnp.ones((SG_CHUNK, SG_CHUNK), dtype=bool))
    w = jnp.where(causal[None], w_s, 0.0)
    mixed = jnp.einsum('gts,bcsgd->bctgd', w, vc) + b_s.T[None, None, :, :, None]
    return u * mixed.reshape(b, s, SG_WIDTH)

def conv_module(a, g, w_dw, b_dw, ln_g, ln_b):
    h = a * jax.nn.sigmoid(g)
    h = lax.conv_general_dilated(h, w_dw[:, None, :], window_strides=(1,),
                                 padding=((CONV_TAPS - 1, 0),),
                                 dimension_numbers=('NWC', 'WIO', 'NWC'),
                                 feature_group_count=CONV_WIDTH) + b_dw
    h = layer_norm(h, ln_g, ln_b)
    return jax.nn.silu(h)

def hybrid_mixer(h, w_in, w_out, sg_ln_g, sg_ln_b, sg_w, sg_b, conv_w, conv_b, conv_ln_g, conv_ln_b):
    b, s, _ = h.shape
    p = h @ w_in
    q = rotary(p[..., Q_OFF:K_OFF].reshape(b, s, ATT_HEADS, HEAD_DIM))
    k = rotary(p[..., K_OFF:V_OFF].reshape(b, s, ATT_HEADS, HEAD_DIM))
    v = p[..., V_OFF:SGU_OFF].reshape(b, s, ATT_HEADS, HEAD_DIM)
    y_att = moba_attention(q, k, v)
    y_sg = spatial_gating(jax.nn.gelu(p[..., SGU_OFF:SGV_OFF]), jax.nn.gelu(p[..., SGV_OFF:CA_OFF]),
                          sg_ln_g, sg_ln_b, sg_w, sg_b)
    y_cv = conv_module(p[..., CA_OFF:CG_OFF], p[..., CG_OFF:IN_COLS], conv_w, conv_b, conv_ln_g, conv_ln_b)
    return jnp.concatenate([y_att, y_sg, y_cv], axis=-1) @ w_out

def grouped_moe(h, w_router, router_bias, w_gate, w_up, w_down):
    b, s, d = h.shape
    hf = h.reshape(b * s, d)
    n = hf.shape[0]
    scores = jax.nn.sigmoid((hf @ w_router).astype(jnp.float32))
    biased = (scores + router_bias.astype(jnp.float32)).reshape(n, N_EXPERT_GROUPS, EXPERTS_PER_GROUP)
    grp_score = jnp.sum(lax.top_k(biased, TOP_K)[0], axis=-1)
    grp = jnp.argmax(grp_score, axis=-1)
    in_grp = jnp.take_along_axis(biased, grp[:, None, None], axis=1)[:, 0]
    _, local = lax.top_k(in_grp, TOP_K)
    expert_ids = grp[:, None] * EXPERTS_PER_GROUP + local
    w_sel = jnp.take_along_axis(scores, expert_ids, axis=1)
    w_sel = w_sel / jnp.sum(w_sel, axis=-1, keepdims=True)
    gates = jnp.sum(jax.nn.one_hot(expert_ids, N_EXPERTS, dtype=jnp.float32) * w_sel[..., None], axis=1)
    gates = gates.astype(hf.dtype)
    out = jnp.zeros_like(hf)
    for e in range(N_EXPERTS):
        y = (jax.nn.silu(hf @ w_gate[e]) * (hf @ w_up[e])) @ w_down[e]
        out = out + gates[:, e:e + 1] * y
    return out.reshape(b, s, d)

def setup_inputs(seed: int = 0) -> dict:
    key = jax.random.key(seed)
    ks = jax.random.split(key, 24)
    f32 = jnp.float32
    nrm = lambda k, shape, sc: jax.random.normal(k, shape, f32) * sc
    gain = lambda k, shape: 1.0 + 0.02 * jax.random.normal(k, shape, f32)
    return {
        "x": jax.random.normal(ks[0], (BATCH, SEQ, D_MODEL), f32),
        "ln_in_g": gain(ks[1], (D_MODEL,)),
        "ln_in_b": nrm(ks[2], (D_MODEL,), 0.02),
        "w_in": nrm(ks[3], (DEPTH, D_MODEL, IN_COLS), D_MODEL ** -0.5),
        "w_out": nrm(ks[4], (DEPTH, MIX_WIDTH, D_MODEL), MIX_WIDTH ** -0.5 * DEEPNORM_BETA),
        "sg_ln_g": gain(ks[5], (DEPTH, SG_WIDTH)),
        "sg_ln_b": nrm(ks[6], (DEPTH, SG_WIDTH), 0.02),
        "sg_w": nrm(ks[7], (DEPTH, SG_GROUPS, SG_CHUNK, SG_CHUNK), SG_CHUNK ** -0.5),
        "sg_b": gain(ks[8], (DEPTH, SG_GROUPS, SG_CHUNK)),
        "conv_w": nrm(ks[9], (DEPTH, CONV_TAPS, CONV_WIDTH), CONV_TAPS ** -0.5),
        "conv_b": nrm(ks[10], (DEPTH, CONV_WIDTH), 0.02),
        "conv_ln_g": gain(ks[11], (DEPTH, CONV_WIDTH)),
        "conv_ln_b": nrm(ks[12], (DEPTH, CONV_WIDTH), 0.02),
        "ln_mix_g": gain(ks[13], (DEPTH, D_MODEL)),
        "ln_mix_b": nrm(ks[14], (DEPTH, D_MODEL), 0.02),
        "w_router": nrm(ks[15], (D_MODEL, N_EXPERTS), D_MODEL ** -0.5),
        "router_bias": nrm(ks[16], (N_EXPERTS,), 0.01),
        "w_gate": nrm(ks[17], (DEPTH, N_EXPERTS, D_MODEL, D_EXPERT), D_MODEL ** -0.5),
        "w_up": nrm(ks[18], (DEPTH, N_EXPERTS, D_MODEL, D_EXPERT), D_MODEL ** -0.5),
        "w_down": nrm(ks[19], (DEPTH, N_EXPERTS, D_EXPERT, D_MODEL), D_EXPERT ** -0.5 * DEEPNORM_BETA),
        "ln_ffn_g": gain(ks[20], (DEPTH, D_MODEL)),
        "ln_ffn_b": nrm(ks[21], (DEPTH, D_MODEL), 0.02),
    }

def reference(x, ln_in_g, ln_in_b, w_in, w_out, sg_ln_g, sg_ln_b, sg_w, sg_b, conv_w, conv_b,
              conv_ln_g, conv_ln_b, ln_mix_g, ln_mix_b, w_router, router_bias, w_gate, w_up, w_down,
              ln_ffn_g, ln_ffn_b):
    h = layer_norm(x, ln_in_g, ln_in_b)
    for l in range(DEPTH):
        mix = hybrid_mixer(h, w_in[l], w_out[l], sg_ln_g[l], sg_ln_b[l], sg_w[l], sg_b[l],
                           conv_w[l], conv_b[l], conv_ln_g[l], conv_ln_b[l])
        h = layer_norm(DEEPNORM_ALPHA * h + mix, ln_mix_g[l], ln_mix_b[l])
        ffn = grouped_moe(h, w_router, router_bias, w_gate[l], w_up[l], w_down[l])
        h = layer_norm(DEEPNORM_ALPHA * h + ffn, ln_ffn_g[l], ln_ffn_b[l])
    return h


_drawn_inputs = setup_inputs


def setup_inputs(seed=0):
    import zlib

    import numpy as np

    out = dict(_drawn_inputs(seed))
    spreads = {}
    factors = {'sg_ln_g': 14.596,
     'sg_ln_b': 17.202,
     'sg_b': 4.627,
     'conv_b': 3.012,
     'conv_ln_g': 4.413,
     'conv_ln_b': 8.0}
    for name, (base, spread) in spreads.items():
        noise = np.random.default_rng([zlib.crc32(name.encode()), seed]).standard_normal(out[name].shape)
        drawn = base * np.exp(spread * noise) if base else spread * noise
        out[name] = __import__('jax').numpy.asarray(drawn.astype(out[name].dtype))
    for name, factor in factors.items():
        out[name] = (out[name] * factor).astype(out[name].dtype)
    return out
```

```python
import math
from contextlib import ExitStack

import numpy as np

import concourse.bass as bass
from concourse import mybir

ALU = mybir.AluOpType
ACT = mybir.ActivationFunctionType
AX_X = mybir.AxisListType.X
F32 = mybir.dt.float32
BF16 = mybir.dt.bfloat16
I32 = mybir.dt.int32

P = 128
SEQ = 256
TB = SEQ // P
D = 1024
KC = D // P
DEPTH = 2
HD = 64
HEADS = 8
ATT = HEADS * HD
SG = 256
GROUPS = 4
CV = 256
CB = CV // P
TAPS = 31
PAD = TAPS - 1
EXPERTS = 16
EGROUPS = 4
PER_GROUP = EXPERTS // EGROUPS
DE = 512
FC = DE // P
PAIRS = EXPERTS // 2
SLOTS = 64
ROUNDS = SEQ // SLOTS
EPS = 1e-5
NEG = -1e30
ALPHA = (2.0 * DEPTH) ** 0.25
SCALE = HD ** -0.5
BANK = 512

UNIT = 4096
RING = 8
SLABS = 5 + 2
PAIR_UNITS = 6
LAYER_UNITS = SLABS + PAIR_UNITS * PAIRS
SLAB_COLS = [2048, 1536, 0, 512, 1024]
BODY = 4
TURNS = BODY * PAIR_UNITS // RING
ITERS = PAIRS // BODY
assert BODY * PAIR_UNITS % RING == 0

T_COS, T_SIN, T_IOTA, T_TIE, T_ID, T_BEFORE, T_MASK = 0, 64, 128, 192, 208, 336, 464
T_COLS = T_MASK + 256
LN_TILES = 4 * TB
ZERO_COLS = 512


def constants():
    t = np.zeros((P, T_COLS), np.float32)
    half = HD // 2
    inv = (10000.0 ** (-np.arange(half, dtype=np.float64) / half)).astype(np.float32)
    ang = np.arange(SEQ, dtype=np.float32)[:, None] * inv[None, :]
    for b in range(TB):
        t[:, T_COS + b * half:T_COS + (b + 1) * half] = np.cos(ang[b * P:(b + 1) * P].astype(np.float64))
        t[:, T_SIN + b * half:T_SIN + (b + 1) * half] = np.sin(ang[b * P:(b + 1) * P].astype(np.float64))
    t[:, T_IOTA:T_IOTA + SLOTS] = np.arange(SLOTS)
    t[:, T_TIE:T_TIE + 16] = (np.arange(4)[None, :] < np.arange(4)[:, None]).reshape(-1)
    r = np.arange(P)
    t[:, T_ID:T_ID + P] = r[:, None] == r[None, :]
    t[:, T_BEFORE:T_BEFORE + P] = r[:, None] < r[None, :]
    t[:, T_MASK + P:T_MASK + 2 * P] = np.where(r[None, :] > r[:, None], np.float32(NEG), np.float32(0))
    return t


def trunk(nc, x, ln_in_g, ln_in_b, w_in, w_out, sg_ln_g, sg_ln_b, sg_w, sg_b, conv_w, conv_b,
          conv_ln_g, conv_ln_b, ln_mix_g, ln_mix_b, w_router, router_bias, w_gate, w_up, w_down,
          ln_ffn_g, ln_ffn_b, table, out):
    with ExitStack() as ctx:
        def sb(name, shape, dt=F32):
            return ctx.enter_context(nc.sbuf_tensor(name, [P] + shape, dt))

        def sem(name):
            return ctx.enter_context(nc.semaphore(name))

        bank = [ctx.enter_context(nc.psum_tensor(f"bank{i}", [P, BANK], F32)) for i in range(8)]

        ring = sb("ring", [RING, UNIT])
        h = sb("h", [TB, D])
        xT = sb("xT", [KC, SEQ])
        mix = sb("mix", [TB, D])
        acc = mix
        area_a = sb("area_a", [3072])
        area_b = sb("area_b", [3072])
        qkT = xT[:, :, :].rearrange("p (i c) t -> p i c t", i=2)
        uv = sb("uv", [TB, 2 * SG])
        v_rows = uv[:, :, :]
        glu = sb("glu", [CB, PAD + SEQ])
        conv = mix[:, 0, 0:CB * SEQ].rearrange("p (c t) -> p c t", c=CB)
        ln_par = sb("ln_par", [2, D])
        sg_ln = sb("sg_ln", [DEPTH, 2, SG])
        cv_ln = sb("cv_ln", [DEPTH, 2, CV])
        sgwT = sb("sgwT", [DEPTH, GROUPS, P])
        sgbT = sb("sgbT", [DEPTH * GROUPS])
        tapsT = sb("tapsT", [CB, DEPTH * TAPS + DEPTH])
        w_rt = sb("w_rt", [KC, EXPERTS])
        r_bias = sb("r_bias", [EXPERTS])
        tab = sb("tab", [T_BEFORE])
        before_bf = sb("before_bf", [P], BF16)
        ones_bf = sb("ones_bf", [P], BF16)
        ident_bf = sb("ident_bf", [P], BF16)
        mask_bf = sb("mask_bf", [2 * P], BF16)
        half_neg = sb("half_neg", [1])
        stats = sb("stats", [2, 6])
        mv = sb("mv", [2])
        n_ln = TB + DEPTH * LN_TILES
        var_eps = sb("var_eps", [n_ln])
        rstd = sb("rstd", [n_ln])
        row_max = sb("row_max", [TB, HEADS])
        neg_max = sb("neg_max", [TB, HEADS])
        row_sum = sb("row_sum", [TB, HEADS])
        row_inv = sb("row_inv", [TB, HEADS])
        rt_e = sb("rt_e", [TB, EXPERTS])
        score = sb("score", [TB, EXPERTS])
        biased = sb("biased", [TB, EXPERTS])
        rank = sb("rank", [TB, EXPERTS])
        sel = sb("sel", [TB, EXPERTS])
        gsum = sb("gsum", [3, TB * EGROUPS])
        mask_row = sb("mask_row", [TB, EXPERTS], BF16)
        wsum = sb("wsum", [2, TB])
        count = sb("count", [1])
        fullest = sb("fullest", [DEPTH], I32)
        slot = sb("slot", [PAIRS, TB, 2])
        gate = sb("gate", [PAIRS, TB, 2])

        qk_rows = area_a[:, 0:2048].rearrange("p (b n) -> p b n", b=TB)
        prob0 = area_a[:, 0:1024].rearrange("p (h k) -> p h k", h=HEADS)
        prob1 = area_a[:, 1024:3072].rearrange("p (h k) -> p h k", h=HEADS)
        by_cos = [area_b[:, i * 1024:i * 1024 + 512] for i in range(2)]
        by_sin = [area_b[:, i * 1024 + 512:i * 1024 + 1024] for i in range(2)]
        probT = area_b[:, :].rearrange("p (g n) -> p g n", g=6)
        xe = area_a[:, 0:1024].rearrange("p (c s) -> p c s", c=KC)
        silu = area_a[:, 1024:1536]
        hid = area_a[:, 1536:2048]
        hidT = area_a[:, 2048:2560].rearrange("p (c s) -> p c s", c=FC)
        y = area_b[:, 0:1024]
        back = [area_b[:, 1024 + 256 * i:1280 + 256 * i].rearrange("p (b t) -> p b t", b=TB) for i in range(2)]
        pick = area_b[:, 1536:1792].rearrange("p (b s) -> p b s", b=TB)
        pick_w = area_b[:, 1792:2048].rearrange("p (b s) -> p b s", b=TB)
        sgw_rows = area_a[:, 0:1024].rearrange("p (n s) -> p n s", n=DEPTH * GROUPS)
        taps_rows = area_a[0:DEPTH * TAPS + DEPTH, 1024:1280]
        sgb_rows = area_a[0:DEPTH * GROUPS, 1280:1408]
        orders = area_b[:, 0:3 * P]
        cmp = area_b[:, 2048:2048 + 2 * TB * EXPERTS * PER_GROUP].rearrange("p (i n) -> p i n", i=2)

        ident = tab[:, T_ID:T_ID + P]
        iota = tab[:, T_IOTA:T_IOTA + SLOTS]
        tie = tab[:, T_TIE:T_TIE + 16].rearrange("p (i j) -> p i j", i=4)

        x_in = sem("x_in")
        table_in = sem("table_in")
        small_in = sem("small_in")
        par_in = sem("par_in")
        out_done = sem("out_done")
        landed = [sem(f"landed{i}") for i in range(RING)]
        used = sem("used")
        casts = sem("casts")
        pool_const = sem("pool_const")
        sgw_masked = sem("sgw_masked")
        setup_pe = sem("setup_pe")
        setup_copied = sem("setup_copied")
        h_ready = sem("h_ready")
        ln_var = sem("ln_var")
        ln_rstd = sem("ln_rstd")
        tr_pe = sem("tr_pe")
        tr_act = sem("tr_act")
        tr_dve = sem("tr_dve")
        sig_ready = sem("sig_ready")
        gelu_ready = sem("gelu_ready")
        sgv_ready = sem("sgv_ready")
        conv_step = sem("conv_step")
        glu_ready = sem("glu_ready")
        convT_pe = sem("convT_pe")
        spatial_pe = sem("spatial_pe")
        conv_ln_done = sem("conv_ln_done")
        conv_out = sem("conv_out")
        sg_out = sem("sg_out")
        rot_products = sem("rot_products")
        rot_done = sem("rot_done")
        v_ready = sem("v_ready")
        qkT_pe = sem("qkT_pe")
        qkT_act = sem("qkT_act")
        qkT_dve = sem("qkT_dve")
        scores_pe = sem("scores_pe")
        max_ready = sem("max_ready")
        exp_done = sem("exp_done")
        probT_pe = sem("probT_pe")
        probT_ready = sem("probT_ready")
        pv_pe = sem("pv_pe")
        att_out = sem("att_out")
        router_pe = sem("router_pe")
        router_exp = sem("router_exp")
        mask_ready = sem("mask_ready")
        before_pe = sem("before_pe")
        routed = sem("routed")
        acc_init = sem("acc_init")
        dve_step = sem("dve_step")
        pool_step = sem("pool_step")

        class Pass:

            def __init__(self, name, used_sem, landed_sems, unit0, used0, pair0, rounds):
                self.unit0 = unit0
                self.load0 = unit0 if rounds == 1 and name == "main" else 0
                self.used0 = used0
                self.pair0 = pair0
                self.rounds = rounds
                self.used = used_sem
                self.landed = landed_sems

        def moe_sems(name):
            return {k: sem(f"{name}_{k}") for k in (
                "pick", "gathered", "pick_t", "xe", "back", "silu", "hid", "hid_t", "hidT", "y", "comb", "added", "renumber")}

        main_sems = moe_sems("moe")
        passes = []
        for l in range(DEPTH):
            m = Pass("main", used, landed, l * LAYER_UNITS + SLABS, l * LAYER_UNITS + SLABS, l * PAIRS, 1)
            m.s = main_sems
            more_used = sem(f"more{l}_used")
            more_landed = [sem(f"more{l}_landed{i}") for i in range(RING)]
            o = Pass("more", more_used, more_landed, l * LAYER_UNITS + SLABS, RING, 0, ROUNDS - 1)
            o.s = moe_sems(f"more{l}")
            passes.append((m, o))

        def unit_at(n):
            return ring[:, n % RING, :]

        def wait_unit(pe, n):
            pe.wait_ge(landed[n % RING], 16 * (n // RING + 1))

        def bcast_row(ap1d, n):
            return ap1d.rearrange("(a n) -> a n", a=1).to_broadcast([P, n])

        block = ctx.enter_context(nc.Block())

        @block.sync
        def _(sp):
            for b in range(TB):
                sp.dma_start(h[:, b, :], x[0, b * P:(b + 1) * P, :]).then_inc(x_in, 16)

            def load_slab(l, i, n):
                if n >= RING:
                    sp.wait_ge(used, n - RING + 1)
                dst = unit_at(n).rearrange("p (c n) -> p c n", c=KC)
                if i < 5:
                    src = w_in[l].rearrange("(p c) n -> p c n", c=KC)[:, :, SLAB_COLS[i]:SLAB_COLS[i] + BANK]
                else:
                    src = w_out[l].rearrange("(p c) n -> p c n", c=KC)[:, :, (i - 5) * BANK:(i - 4) * BANK]
                sp.dma_start(dst, src).then_inc(landed[n % RING], 16)

            def load_pairs(l, ps, rnd, it):
                for j in range(BODY):
                    first = it * (2 * BODY) + 2 * j
                    for u in range(PAIR_UNITS):
                        k = PAIR_UNITS * j + u
                        turn = rnd * (ITERS * BODY * PAIR_UNITS) + it * (BODY * PAIR_UNITS)
                        sp.wait_ge(ps.used, turn + (ps.used0 + k - RING + 1))
                        half = u // 2 if u < 4 else u - 4
                        if u < 4:
                            w = (w_gate, w_up)[u % 2][l].rearrange("e (p c) n -> p e (c n)", c=KC)
                        else:
                            w = w_down[l].rearrange("e (p c) n -> p e (c n)", c=FC)
                        src = w[:, bass.ds(first, 2), half * 2048:(half + 1) * 2048]
                        at = (ps.unit0 + k) % RING
                        sp.dma_start(ring[:, at, :].rearrange("p (e n) -> p e n", e=2), src)\
                          .then_inc(ps.landed[at], 16)

            for l in range(DEPTH):
                main, more = passes[l]
                for i in range(SLABS):
                    load_slab(l, i, l * LAYER_UNITS + i)
                with sp.Fori(0, ITERS) as it:
                    load_pairs(l, main, 0, it)
                sp.wait_ge(routed, l + 1)
                n = sp.value_load(fullest[0:1, l:l + 1], min_val=0, max_val=SEQ)
                with sp.If(n > SLOTS):
                    sp.wait_ge(used, (l + 1) * LAYER_UNITS)
                    sp.sem_inc(more.used, RING)
                    with sp.Fori(0, ROUNDS - 1) as rnd:
                        with sp.Fori(0, ITERS) as it:
                            load_pairs(l, more, rnd, it)
                    sp.wait_ge(more.used, RING + (ROUNDS - 1) * PAIRS * PAIR_UNITS)
            for b in range(TB):
                sp.wait_ge(h_ready, 2 * TB * DEPTH + b + 1)
                sp.dma_start(out[0, b * P:(b + 1) * P, :], h[:, b, :]).then_inc(out_done, 16)
            sp.wait_ge(out_done, 16 * TB)

        @block.tensor
        def _(pe):
            pe.wait_ge(table_in, 32)
            pe.wait_ge(small_in, 16 * 10)
            pe.wait_ge(sgw_masked, 1)
            for n in range(DEPTH * GROUPS):
                mm = pe.transpose(bank[n // 4][:, (n % 4) * P:(n % 4 + 1) * P], sgw_rows[:, n, :], ident)
                if n % 4 == 3:
                    mm.then_inc(setup_pe, 1)
            nt = DEPTH * TAPS + DEPTH
            for cb in range(CB):
                pe.transpose(bank[2][:, cb * nt:(cb + 1) * nt], taps_rows[:, cb * P:(cb + 1) * P],
                             ident[0:nt, 0:nt])
            pe.transpose(bank[2][:, 256:256 + DEPTH * GROUPS], sgb_rows,
                         ident[0:DEPTH * GROUPS, 0:DEPTH * GROUPS]).then_inc(setup_pe, 1)
            pe.wait_ge(setup_copied, 1)

            def turn(src, b, stage):
                for half in range(2):
                    dst = bank[2 * b + half]
                    for c in range(4):
                        mm = pe.transpose(dst[:, c * P:(c + 1) * P], src[:, b, 4 * half + c::KC], ident)
                    mm.then_inc(tr_pe, 1)

            def wait_xT(stage):
                pe.wait_ge(tr_act, 2 * (stage + 1))
                pe.wait_ge(tr_dve, 2 * (stage + 1))

            def rows_slab(n, banks):
                wait_unit(pe, n)
                w = unit_at(n).rearrange("p (c n) -> p c n", c=KC)
                for b in range(TB):
                    for c in range(KC):
                        mm = pe.matmul(bank[banks[b]][:, :], xT[:, c, b * P:(b + 1) * P], w[:, c, :],
                                       start=c == 0, stop=c == KC - 1)
                    if b == TB - 1:
                        mm.then_inc(used, 1)

            def experts(l, ps, rnd, it):
                s = ps.s
                pairs_before = rnd * PAIRS + it * BODY

                def nth(name, j, k=1, per=1):
                    pe.wait_ge(s[name], pairs_before * per + ((ps.pair0 + j) * per + k))

                def landed_unit(k):
                    at = (ps.unit0 + k) % RING
                    turns = rnd * (ITERS * TURNS * 16) + it * (TURNS * 16)
                    pe.wait_ge(ps.landed[at], turns + 16 * ((ps.load0 + k) // RING + 1))
                    return ring[:, at, :]

                def gather(j):
                    nth("pick", j, 1, 2)
                    for c in range(KC):
                        for b in range(TB):
                            mm = pe.matmul(bank[c // 4][:, (c % 4) * P:(c % 4 + 1) * P], h[:, b, c::KC],
                                           pick[:, b, :], start=b == 0, stop=b == TB - 1)
                        if c % 4 == 3:
                            mm.then_inc(s["gathered"], 1)
                    nth("pick", j, 2, 2)
                    if j >= 2:
                        nth("added", j - 2, 3, 4)
                    elif j == 1:
                        nth("back", 0)
                    for b in range(TB):
                        mm = pe.transpose(bank[7][:, b * P:(b + 1) * P], pick_w[:, b, :], ident)
                    mm.then_inc(s["pick_t"], 1)

                def gate_up(j):
                    nth("xe", j, 2, 2)
                    for u in range(4):
                        w = landed_unit(PAIR_UNITS * j + u).rearrange("p (e c n) -> p e c n", e=2, c=4)
                        for c in range(4):
                            for e in range(2):
                                k = 4 * (u // 2) + c
                                mm = pe.matmul(bank[2 + u % 2][e * SLOTS:(e + 1) * SLOTS, :],
                                               xe[:, k, e * SLOTS:(e + 1) * SLOTS], w[:, e, c, :],
                                               start=k == 0, stop=k == KC - 1)
                        mm.then_inc(ps.used, 1)

                def turn_hid(j):
                    nth("hid", j)
                    if j >= 1:
                        nth("added", j - 1, 4, 4)
                    for c in range(FC):
                        mm = pe.transpose(bank[4][:, c * P:(c + 1) * P], hid[:, c::FC], ident)
                    mm.then_inc(s["hid_t"], 1)

                def down(j):
                    nth("hidT", j)
                    for u in range(2):
                        w = landed_unit(PAIR_UNITS * j + 4 + u).rearrange("p (e c n) -> p e c n", e=2, c=2)
                        for n in range(2):
                            for c in range(2):
                                for e in range(2):
                                    k = 2 * u + c
                                    mm = pe.matmul(bank[5 + n][e * SLOTS:(e + 1) * SLOTS, :],
                                                   hidT[:, k, e * SLOTS:(e + 1) * SLOTS],
                                                   w[:, e, c, n * BANK:(n + 1) * BANK],
                                                   start=k == 0, stop=k == FC - 1)
                        mm.then_inc(ps.used, 1)

                def combine(j):
                    nth("y", j, 2, 2)
                    nth("back", min(j + 1, BODY - 1))
                    for k in range(4):
                        b, n = k // 2, k % 2
                        if k >= 2:
                            nth("added", j, k - 1, 4)
                        mm = pe.matmul(bank[(7, 4)[k % 2]][:, :], back[j % 2][:, b, :],
                                       y[:, n * BANK:(n + 1) * BANK], start=True, stop=True)
                        mm.then_inc(s["comb"], 1)

                gather(0)
                for j in range(BODY):
                    gate_up(j)
                    if j:
                        combine(j - 1)
                    if j < BODY - 1:
                        gather(j + 1)
                    turn_hid(j)
                    down(j)
                combine(BODY - 1)
                nth("added", BODY - 1, 4, 4)

            for l in range(DEPTH):
                u0 = l * LAYER_UNITS
                for b in range(TB):
                    pe.wait_ge(h_ready, 2 * TB * l + b + 1)
                    turn(h, b, 3 * l)
                wait_xT(3 * l)
                wait_unit(pe, u0)
                w = unit_at(u0).rearrange("p (c n) -> p c n", c=KC)
                for k in (2, 3, 0, 1):
                    for c in range(KC):
                        mm = pe.matmul(bank[4 + k // 2][:, (k % 2) * SEQ:(k % 2 + 1) * SEQ],
                                       w[:, c, k * P:(k + 1) * P], xT[:, c, :], start=c == 0, stop=c == KC - 1)
                mm.then_inc(used, 1)
                rows_slab(u0 + 1, (6, 7))
                rows_slab(u0 + 2, (0, 1))
                pe.wait_ge(gelu_ready, TB * (l + 1))
                pe.wait_ge(conv_step, CB * TAPS * (l + 1))
                for b in range(TB):
                    for cb in range(CB):
                        mm = pe.transpose(bank[7][:, b * CV + cb * P:b * CV + (cb + 1) * P],
                                          conv[:, cb, b * P:(b + 1) * P], ident)
                mm.then_inc(convT_pe, 1)
                for b in range(TB):
                    pe.wait_ge(sgv_ready, TB * l + b + 1)
                    for g in range(GROUPS):
                        mm = pe.matmul(bank[6][:, b * SG + g * HD:b * SG + (g + 1) * HD], sgwT[:, l, g, :],
                                       uv[:, b, SG + g * HD:SG + (g + 1) * HD], start=True, stop=True)
                mm.then_inc(spatial_pe, 1)
                rows_slab(u0 + 3, (2, 3))
                rows_slab(u0 + 4, (4, 5))
                for b in range(TB):
                    for i in range(2):
                        pe.wait_ge(rot_done, 2 * TB * l + 2 * i + b + 1)
                        for hp in range(HEADS // 2):
                            mm = pe.transpose(bank[2 * i + b][:, hp * P:(hp + 1) * P],
                                              qk_rows[:, b, i * ATT + hp * P:i * ATT + (hp + 1) * P], ident)
                        mm.then_inc(qkT_pe, 1)
                pe.wait_ge(v_ready, TB * (l + 1))
                pe.wait_ge(qkT_act, 2 * l + 1)
                pe.wait_ge(qkT_dve, 2 * l + 1)
                for par in range(2):
                    pe.matmul(bank[4 + par][:, :], ident_bf[:, :],
                              mask_bf[:, P:2 * P].unsqueeze(1).to_broadcast([P, 4, P]), start=True, stop=False,
                              skip_group_check=True)
                for hp in range(HEADS // 2):
                    for par in range(2):
                        q = slice(par * HD, (par + 1) * HD)
                        mm = pe.matmul(bank[4 + par][:, hp * P:(hp + 1) * P], qkT[q, 0, hp, 0:P], qkT[q, 1, hp, 0:P],
                                       start=False, stop=True, skip_group_check=True)
                        if hp == HEADS // 2 - 1:
                            mm.then_inc(scores_pe, 1)
                pe.wait_ge(qkT_act, 2 * (l + 1))
                pe.wait_ge(qkT_dve, 2 * (l + 1))
                for i in range(4):
                    pe.matmul(bank[i][:, :], ident_bf[:, :],
                              mask_bf[:, :].unsqueeze(1).to_broadcast([P, 2, 2 * P]), start=True, stop=False,
                              skip_group_check=True)
                for hp in range(HEADS // 2):
                    for par in range(2):
                        q = slice(par * HD, (par + 1) * HD)
                        mm = pe.matmul(bank[2 * (hp // 2) + par][:, (hp % 2) * SEQ:(hp % 2 + 1) * SEQ],
                                       qkT[q, 0, hp, P:2 * P], qkT[q, 1, hp, :],
                                       start=False, stop=True, skip_group_check=True)
                        if hp % 2 == 1:
                            mm.then_inc(scores_pe, 1)
                pe.wait_ge(exp_done, 2 * HEADS * l + HEADS)
                for g in range(2):
                    for i in range(4):
                        mm = pe.transpose(bank[4 + g][:, i * P:(i + 1) * P], prob0[:, 4 * g + i, :], ident)
                    mm.then_inc(probT_pe, 1)
                for g in range(4):
                    pe.wait_ge(exp_done, 2 * HEADS * l + HEADS + 4 * (g // 2 + 1))
                    for i in range(4):
                        mm = pe.transpose(bank[g][:, i * P:(i + 1) * P],
                                          prob1[:, 2 * g + i // 2, (i % 2) * P:(i % 2 + 1) * P], ident)
                    mm.then_inc(probT_pe, 1)
                pe.wait_ge(sg_out, l + 1)
                for hd in range(HEADS):
                    if hd % 4 == 0:
                        pe.wait_ge(probT_ready, 6 * l + hd // 4 + 1)
                    mm = pe.matmul(bank[6][:, hd * HD:(hd + 1) * HD], probT[:, hd // 4, (hd % 4) * P:(hd % 4 + 1) * P],
                                   v_rows[:, 0, hd * HD:(hd + 1) * HD], start=True, stop=True)
                mm.then_inc(pv_pe, 1)
                for hd in range(HEADS):
                    if hd % 2 == 0:
                        pe.wait_ge(probT_ready, 6 * l + 2 + hd // 2 + 1)
                    for kb in range(TB):
                        i = 2 * (hd % 2) + kb
                        mm = pe.matmul(bank[7][:, hd * HD:(hd + 1) * HD], probT[:, 2 + hd // 2, i * P:(i + 1) * P],
                                       v_rows[:, kb, hd * HD:(hd + 1) * HD], start=kb == 0, stop=kb == 1)
                mm.then_inc(pv_pe, 1)
                pe.wait_ge(conv_out, l + 1)
                for b in range(TB):
                    pe.wait_ge(att_out, TB * l + b + 1)
                    turn(mix, b, 3 * l + 1)
                wait_xT(3 * l + 1)
                rows_slab(u0 + 5, (4, 6))
                rows_slab(u0 + 6, (5, 7))
                for b in range(TB):
                    pe.wait_ge(h_ready, 2 * TB * l + TB + b + 1)
                    turn(h, b, 3 * l + 2)
                wait_xT(3 * l + 2)
                for b in range(TB):
                    for c in range(KC):
                        mm = pe.matmul(bank[4][:, b * EXPERTS:(b + 1) * EXPERTS], xT[:, c, b * P:(b + 1) * P],
                                       w_rt[:, c, :], start=c == 0, stop=c == KC - 1)
                mm.then_inc(router_pe, 1)
                pe.wait_ge(mask_ready, l + 1)
                pe.matmul(bank[5][:, 0:16], before_bf[:, :], mask_row[:, 0, :], start=True, stop=True)
                pe.matmul(bank[5][:, 16:32], ones_bf[:, :], mask_row[:, 0, :], start=True, stop=False)
                pe.matmul(bank[5][:, 16:32], before_bf[:, :], mask_row[:, 1, :], start=False, stop=True)
                pe.matmul(bank[5][:, 32:48], ones_bf[:, :], mask_row[:, 0, :], start=True, stop=False)
                pe.matmul(bank[5][:, 32:48], ones_bf[:, :], mask_row[:, 1, :], start=False, stop=True)\
                  .then_inc(before_pe, 1)
                main, more = passes[l]
                with pe.Fori(0, ITERS) as it:
                    experts(l, main, 0, it)
                pe.wait_ge(routed, l + 1)
                n = pe.value_load(fullest[0:1, l:l + 1], min_val=0, max_val=SEQ)
                with pe.If(n > SLOTS):
                    with pe.Fori(0, ROUNDS - 1) as rnd:
                        with pe.Fori(0, ITERS) as it:
                            experts(l, more, rnd, it)

        @block.scalar
        def _(act):
            act.dma_start(tab[:, :], table[:, 0:T_BEFORE]).then_inc(table_in, 16)
            act.dma_start(orders, table[:, T_BEFORE:T_COLS]).then_inc(table_in, 16)
            act.dma_start(ln_par[:, 0, :], bcast_row(ln_in_g, D)).then_inc(par_in, 16)
            act.dma_start(ln_par[:, 1, :], bcast_row(ln_in_b, D)).then_inc(par_in, 16)
            act.dma_start(sgw_rows, sg_w.rearrange("l g t s -> t (l g) s")).then_inc(small_in, 16)
            act.dma_start(taps_rows[0:DEPTH * TAPS, :], conv_w.rearrange("l k c -> (l k) c")).then_inc(small_in, 16)
            act.dma_start(taps_rows[DEPTH * TAPS:, :], conv_b).then_inc(small_in, 16)
            act.dma_start(sgb_rows, sg_b.rearrange("l g t -> (l g) t")).then_inc(small_in, 16)
            act.dma_start(w_rt[:, :, :], w_router.rearrange("(p c) n -> p c n", c=KC)).then_inc(small_in, 16)
            act.dma_start(r_bias[:, :], bcast_row(router_bias, EXPERTS)).then_inc(small_in, 16)
            for dst, g, s in ((sg_ln, sg_ln_g, sg_ln_b), (cv_ln, conv_ln_g, conv_ln_b)):
                for i, src in enumerate((g, s)):
                    act.dma_start(dst[:, :, i, :], src.rearrange("(a l) n -> a l n", a=1).to_broadcast([P, DEPTH, SG]))\
                       .then_inc(small_in, 16)

            def next_params(n, gain, shift, free_after):
                act.wait_ge(h_ready, free_after)
                act.dma_start(ln_par[:, 0, :], bcast_row(gain, D)).then_inc(par_in, 16)
                act.dma_start(ln_par[:, 1, :], bcast_row(shift, D)).then_inc(par_in, 16)

            def copy_columns(stage):
                for b in range(TB):
                    act.wait_ge(tr_pe, 4 * stage + 2 * b + 1)
                    act.activation(xT[:, 0:4, b * P:(b + 1) * P],
                                   bank[2 * b][:, :].rearrange("p (c t) -> p c t", c=4), ACT.Copy).then_inc(tr_act, 1)

            def experts(l, ps, rnd, it):
                s = ps.s
                pairs_before = rnd * PAIRS + it * BODY
                units_before = pairs_before * PAIR_UNITS

                def nth(name, j, k=1, per=1):
                    act.wait_ge(s[name], pairs_before * per + ((ps.pair0 + j) * per + k))

                def tokens(j):
                    for half in range(2):
                        nth("gathered", j, half + 1, 2)
                        act.activation(xe[:, 4 * half:4 * half + 4, :],
                                       bank[half][:, :].rearrange("p (c s) -> p c s", c=4), ACT.Copy)\
                           .then_inc(s["xe"], 1)
                    nth("pick_t", j)
                    act.activation(back[j % 2], bank[7][:, 0:SEQ].rearrange("p (b t) -> p b t", b=TB), ACT.Copy)\
                       .then_inc(s["back"], 1)

                tokens(0)
                for j in range(BODY):
                    act.wait_ge(ps.used, units_before + (ps.used0 + PAIR_UNITS * j + 4))
                    act.activation(silu, bank[2][:, :], ACT.Silu).then_inc(s["silu"], 1)
                    if j < BODY - 1:
                        tokens(j + 1)
                    act.wait_ge(ps.used, units_before + (ps.used0 + PAIR_UNITS * (j + 1)))
                    for n in range(2):
                        act.activation(y[:, n * BANK:(n + 1) * BANK], bank[5 + n][:, :], ACT.Copy)\
                           .then_inc(s["y"], 1)

            for l in range(DEPTH):
                next_params(2 * l + 1, ln_mix_g[l], ln_mix_b[l], 2 * TB * l + TB)
                copy_columns(3 * l)
                act.wait_ge(used, l * LAYER_UNITS + 1)
                act.activation(prob1[:, 0:2, :], bank[5][:, :].rearrange("p (h k) -> p h k", h=2), ACT.Sigmoid)\
                   .then_inc(sig_ready, 1)
                act.wait_ge(used, l * LAYER_UNITS + 2)
                for b in range(TB):
                    act.activation(uv[:, b, :], bank[6 + b][:, :], ACT.Gelu_apprx_tanh).then_inc(gelu_ready, 1)
                act.wait_ge(conv_ln_done, TB * (l + 1))
                act.activation(mix[:, :, ATT + SG:D], mix[:, :, ATT + SG:D], ACT.Silu).then_inc(conv_out, 1)
                act.wait_ge(used, l * LAYER_UNITS + 5)
                act.wait_ge(sg_out, l + 1)
                for b in range(TB):
                    act.activation(v_rows[:, b, :], bank[4 + b][:, :], ACT.Copy).then_inc(v_ready, 1)
                for b in range(TB):
                    act.wait_ge(qkT_pe, 4 * l + 2 * b + 1)
                    act.activation(qkT[:, 0, :, b * P:(b + 1) * P],
                                   bank[b][:, :].rearrange("p (c t) -> p c t", c=4), ACT.Copy).then_inc(qkT_act, 1)
                for qb in range(TB):
                    act.wait_ge(max_ready, TB * l + qb + 1)
                    for hd in range(HEADS):
                        if qb == 0:
                            src, dst = bank[4 + hd % 2][:, (hd // 2) * P:(hd // 2 + 1) * P], prob0[:, hd, :]
                        else:
                            src = bank[2 * (hd // 4) + hd % 2][:, (hd // 2 % 2) * SEQ:(hd // 2 % 2 + 1) * SEQ]
                            dst = prob1[:, hd, :]
                        act.activation(dst, src, ACT.Exp, bias=neg_max[:, qb, hd:hd + 1], scale=SCALE,
                                       accum_out=row_sum[:, qb, hd:hd + 1]).then_inc(exp_done, 1)
                copy_columns(3 * l + 1)
                copy_columns(3 * l + 2)
                next_params(2 * l + 2, ln_ffn_g[l], ln_ffn_b[l], 2 * TB * l + 2 * TB)
                act.wait_ge(router_pe, l + 1)
                act.activation(rt_e[:, :, :], bank[4][:, 0:TB * EXPERTS].rearrange("p (b e) -> p b e", b=TB),
                               ACT.Exp, scale=-1.0).then_inc(router_exp, 1)
                main, more = passes[l]
                with act.Fori(0, ITERS) as it:
                    experts(l, main, 0, it)
                act.wait_ge(routed, l + 1)
                n = act.value_load(fullest[0:1, l:l + 1], min_val=0, max_val=SEQ)
                with act.If(n > SLOTS):
                    with act.Fori(0, ROUNDS - 1) as rnd:
                        with act.Fori(0, ITERS) as it:
                            experts(l, more, rnd, it)

        @block.gpsimd
        def _(pool):
            steps = [0]

            def step(ins):
                steps[0] += 1
                ins.then_inc(pool_step, 1)
                pool.wait_ge(pool_step, steps[0])

            pool.memset(half_neg[:, :], -0.5).then_inc(pool_const, 1)
            pool.memset(ones_bf[:, :], 1.0).then_inc(pool_const, 1)
            pool.memset(glu[:, :, 0:PAD], 0.0).then_inc(pool_const, 1)
            pool.wait_ge(small_in, 16 * 10)
            pool.affine_select(out=sgw_rows, in_=sgw_rows, compare_op=ALU.is_ge, fill=0.0, base=0,
                               pattern=[[0, DEPTH * GROUPS], [-1, P]], channel_multiplier=1).then_inc(sgw_masked, 1)
            pool.wait_ge(pool_const, 3)
            norms = [0]

            def inverse_deviations(n):
                for _ in range(n):
                    i = norms[0]
                    norms[0] += 1
                    pool.wait_ge(ln_var, i + 1)
                    pool.tensor_tensor(rstd[:, i:i + 1], var_eps[:, i:i + 1], half_neg[:, :], ALU.pow)\
                        .then_inc(ln_rstd, 1)

            def rotate(l, i):
                for b in range(TB):
                    pool.wait_ge(rot_products, 2 * TB * l + 2 * i + b + 1)
                    a = by_cos[b].rearrange("p (h x d) -> p h x d", h=HEADS, x=2)
                    s = by_sin[b].rearrange("p (h x d) -> p h x d", h=HEADS, x=2)
                    o = qk_rows[:, b, i * ATT:(i + 1) * ATT].rearrange("p (h x d) -> p h x d", h=HEADS, x=2)
                    pool.tensor_tensor(o[:, :, 0, :], a[:, :, 0, :], s[:, :, 1, :], ALU.subtract)
                    pool.tensor_tensor(o[:, :, 1, :], a[:, :, 1, :], s[:, :, 0, :], ALU.add).then_inc(rot_done, 1)

            inverse_deviations(TB)
            for l in range(DEPTH):
                inverse_deviations(TB)
                rotate(l, 0)
                inverse_deviations(TB)
                rotate(l, 1)
                inverse_deviations(TB)
                for b in range(TB):
                    pool.wait_ge(h_ready, 2 * TB * l + TB + b + 1)
                    pool.tensor_scalar(acc[:, b, :], h[:, b, :], ALPHA, 1.0, ALU.mult, ALU.mult).then_inc(acc_init, 1)
                inverse_deviations(TB)

        @block.vector
        def _(dve):
            steps = [0]

            def step(ins):
                steps[0] += 1
                ins.then_inc(dve_step, 1)
                dve.wait_ge(dve_step, steps[0])

            norms = [0]

            def layer_norm(src, dst, gain, shift, width, signal):
                i = norms[0]
                norms[0] += 1
                parts = max(1, width // BANK)
                w = width // parts
                for k in range(parts):
                    ins = dve.bn_stats(stats[:, k, :], src[:, k * w:(k + 1) * w])
                step(ins)
                step(dve.bn_aggr(mv[:, :], stats[:, 0:parts, :]))
                dve.tensor_scalar(var_eps[:, i:i + 1], mv[:, 1:2], EPS, None, ALU.add).then_inc(ln_var, 1)
                step(dve.scalar_tensor_tensor(out=dst, in0=src, scalar=mv[:, 0:1], in1=gain,
                                              op0=ALU.subtract, op1=ALU.mult))
                dve.wait_ge(ln_rstd, i + 1)
                dve.scalar_tensor_tensor(out=dst, in0=dst, scalar=rstd[:, i:i + 1], in1=shift,
                                         op0=ALU.mult, op1=ALU.add).then_inc(signal, 1)

            def copy_columns(stage):
                for b in range(TB):
                    dve.wait_ge(tr_pe, 4 * stage + 2 * b + 2)
                    dve.tensor_copy(xT[:, 4:8, b * P:(b + 1) * P],
                                    bank[2 * b + 1][:, :].rearrange("p (c t) -> p c t", c=4)).then_inc(tr_dve, 1)

            def rotary_products(l, i):
                for b in range(TB):
                    src = bank[2 * i + b][:, :].rearrange("p (h d) -> p h d", d=HD // 2)
                    if i == 1:
                        dve.wait_ge(rot_done, 2 * TB * l + b + 1)
                    elif l:
                        pass
                    for t0, dst in ((T_COS, by_cos[b]), (T_SIN, by_sin[b])):
                        angle = tab[:, t0 + b * 32:t0 + (b + 1) * 32].unsqueeze(1).to_broadcast([P, 16, 32])
                        ins = dve.tensor_tensor(dst.rearrange("p (h d) -> p h d", d=HD // 2), src, angle, ALU.mult)
                    ins.then_inc(rot_products, 1)

            def routing(l):
                sc = score[:, :, :].rearrange("p b e -> p (b e)")
                bi = biased[:, :, :].rearrange("p b e -> p (b e)")
                se = sel[:, :, :].rearrange("p b e -> p (b e)")
                ra = rank[:, :, :].rearrange("p b e -> p (b e)")
                ex = rt_e[:, :, :].rearrange("p b e -> p (b e)")
                dve.wait_ge(router_exp, l + 1)
                step(dve.tensor_scalar(ex, ex, 1.0, None, ALU.add))
                step(dve.reciprocal(sc, ex))
                step(dve.tensor_tensor(biased[:, :, :], score[:, :, :],
                                       r_bias[:, :].unsqueeze(1).to_broadcast([P, TB, EXPERTS]), ALU.add))

                def ranks(v, n, m, dst):
                    them = v.rearrange("p (g j) -> p g j", j=m).unsqueeze(2).to_broadcast([P, n, m, m])
                    one = v.rearrange("p (g j) -> p g j", j=m).unsqueeze(3).to_broadcast([P, n, m, m])
                    c0 = cmp[:, 0, 0:n * m * m].rearrange("p (g i j) -> p g i j", i=m, j=m)
                    c1 = cmp[:, 1, 0:n * m * m].rearrange("p (g i j) -> p g i j", i=m, j=m)
                    dve.tensor_tensor(c0, them, one, ALU.is_gt)
                    step(dve.tensor_tensor(c1, them, one, ALU.is_equal))
                    step(dve.tensor_tensor(c1, c1, tie.unsqueeze(1).to_broadcast([P, n, m, m]), ALU.mult))
                    step(dve.tensor_tensor(c0, c0, c1, ALU.add))
                    step(dve.tensor_reduce(dst, c0, AX_X, ALU.add))

                ranks(bi, TB * EGROUPS, PER_GROUP, ra.rearrange("p (g j) -> p g j", j=PER_GROUP))
                step(dve.tensor_scalar(se, ra, 2.0, None, ALU.is_lt))
                step(dve.tensor_tensor(ra, se, bi, ALU.mult))
                step(dve.tensor_reduce(gsum[:, 0, :], ra.rearrange("p (g j) -> p g j", j=PER_GROUP), AX_X, ALU.add))
                ranks(gsum[:, 0, :], TB, EGROUPS, gsum[:, 1, :].rearrange("p (g j) -> p g j", j=EGROUPS))
                step(dve.tensor_scalar(gsum[:, 2, :], gsum[:, 1, :], 1.0, None, ALU.is_lt))
                step(dve.tensor_tensor(se.rearrange("p (g j) -> p g j", j=PER_GROUP),
                                       se.rearrange("p (g j) -> p g j", j=PER_GROUP),
                                       gsum[:, 2, :].unsqueeze(2).to_broadcast([P, TB * EGROUPS, PER_GROUP]), ALU.mult))
                dve.tensor_copy(mask_row[:, :, :], sel[:, :, :]).then_inc(mask_ready, 1)
                step(dve.tensor_tensor(ra, se, sc, ALU.mult))
                step(dve.tensor_reduce(wsum[:, 0, :], rank[:, :, :], AX_X, ALU.add))
                step(dve.reciprocal(wsum[:, 1, :], wsum[:, 0, :]))
                for b in range(TB):
                    dve.tensor_scalar(gate[:, :, b, :], rank[:, b, :].rearrange("p (i e) -> p i e", e=2),
                                      wsum[:, 1, b:b + 1], None, ALU.mult)
                numbered = cmp[:, 0, 0:TB * EXPERTS].rearrange("p (b e) -> p b e", b=TB)
                dve.wait_ge(before_pe, l + 1)
                for b in range(TB):
                    ins = dve.scalar_tensor_tensor(out=numbered[:, b, :], in0=bank[5][:, b * 16:(b + 1) * 16], scalar=1.0,
                                                   in1=sel[:, b, :], op0=ALU.add, op1=ALU.mult)
                step(ins)
                for b in range(TB):
                    dve.tensor_scalar(slot[:, :, b, :], numbered[:, b, :].rearrange("p (i e) -> p i e", e=2),
                                      -1.0, None, ALU.add)
                step(dve.tensor_reduce(count[:, :], bank[5][:, 32:48], AX_X, ALU.max))
                dve.tensor_copy(fullest[:, l:l + 1], count[:, :]).then_inc(routed, 1)
                dve.wait_ge(routed, l + 1)

            def experts(l, ps, rnd, it):
                s = ps.s
                pairs_before = rnd * PAIRS + it * BODY
                units_before = pairs_before * PAIR_UNITS

                def nth(name, j, k=1, per=1):
                    dve.wait_ge(s[name], pairs_before * per + ((ps.pair0 + j) * per + k))

                def picks(j):
                    if j:
                        nth("pick_t", j - 1)
                    elif ps.rounds > 1:
                        dve.wait_ge(s["renumber"], rnd + 1)
                    pair = it * BODY + j
                    nums = slot[:, bass.ds(pair, 1), :, :].rearrange("p i b e -> p (i b e)")
                    wts = gate[:, bass.ds(pair, 1), :, :].rearrange("p i b e -> p (i b e)")
                    p3 = pick.rearrange("p b (e s) -> p (b e) s", e=2)
                    w3 = pick_w.rearrange("p b (e s) -> p (b e) s", e=2)
                    dve.tensor_tensor(p3, iota.unsqueeze(1).to_broadcast([P, 4, SLOTS]),
                                      nums.unsqueeze(2).to_broadcast([P, 4, SLOTS]), ALU.is_equal)\
                       .then_inc(s["pick"], 1)
                    nth("pick", j, 1, 2)
                    dve.tensor_tensor(w3, p3, wts.unsqueeze(2).to_broadcast([P, 4, SLOTS]), ALU.mult)\
                       .then_inc(s["pick"], 1)

                def add_back(j):
                    for k in range(4):
                        b, n = k // 2, k % 2
                        nth("comb", j, k + 1, 4)
                        a = acc[:, b, n * BANK:(n + 1) * BANK]
                        dve.tensor_tensor(a, a, bank[(7, 4)[k % 2]][:, :], ALU.add).then_inc(s["added"], 1)

                picks(0)
                for j in range(BODY):
                    if j < BODY - 1:
                        picks(j + 1)
                    nth("silu", j)
                    dve.tensor_tensor(hid, silu, bank[3][:, :], ALU.mult).then_inc(s["hid"], 1)
                    if j:
                        add_back(j - 1)
                    nth("hid_t", j)
                    dve.tensor_copy(hidT, bank[4][:, :].rearrange("p (c s) -> p c s", c=FC)).then_inc(s["hidT"], 1)
                add_back(BODY - 1)
                nth("added", BODY - 1, 4, 4)

            dve.wait_ge(table_in, 32)
            dve.tensor_copy(before_bf[:, :], orders[:, 0:P]).then_inc(casts, 1)
            dve.tensor_copy(ident_bf[:, :], ident).then_inc(casts, 1)
            dve.tensor_copy(mask_bf[:, :], orders[:, P:3 * P]).then_inc(casts, 1)
            dve.wait_ge(casts, 3)
            dve.wait_ge(par_in, 32)
            dve.wait_ge(x_in, 16 * TB)
            for b in range(TB):
                layer_norm(h[:, b, :], h[:, b, :], ln_par[:, 0, :], ln_par[:, 1, :], D, h_ready)
            dve.wait_ge(setup_pe, DEPTH + 1)
            for l in range(DEPTH):
                dve.tensor_copy(sgwT[:, l, :, :], bank[l][:, :].rearrange("p (g t) -> p g t", g=GROUPS))
            nt = DEPTH * TAPS + DEPTH
            dve.tensor_copy(tapsT[:, :, :], bank[2][:, 0:CB * nt].rearrange("p (c k) -> p c k", c=CB))
            dve.tensor_copy(sgbT[:, :], bank[2][:, 256:256 + DEPTH * GROUPS]).then_inc(setup_copied, 1)
            dve.wait_ge(setup_copied, 1)
            dve.wait_ge(pool_const, 3)

            for l in range(DEPTH):
                copy_columns(3 * l)
                dve.wait_ge(sig_ready, l + 1)
                dve.tensor_tensor(glu[:, :, PAD:PAD + SEQ], bank[4][:, :].rearrange("p (c t) -> p c t", c=CB),
                                  prob1[:, 0:2, :], ALU.mult).then_inc(glu_ready, 1)
                dve.wait_ge(glu_ready, l + 1)
                for k in range(TAPS):
                    for cb in range(CB):
                        n = CB * k + cb
                        tap = tapsT[:, cb, l * TAPS + k:l * TAPS + k + 1]
                        src = glu[:, cb, k:k + SEQ]
                        if k == 0:
                            ins = dve.tensor_scalar(conv[:, cb, :], src, tap,
                                                    tapsT[:, cb, DEPTH * TAPS + l:DEPTH * TAPS + l + 1], ALU.mult, ALU.add)
                        else:
                            dve.wait_ge(conv_step, CB * TAPS * l + n - 1)
                            ins = dve.scalar_tensor_tensor(out=conv[:, cb, :], in0=src, scalar=tap,
                                                           in1=conv[:, cb, :], op0=ALU.mult, op1=ALU.add)
                        ins.then_inc(conv_step, 1)
                for b in range(TB):
                    dve.wait_ge(gelu_ready, TB * l + b + 1)
                    layer_norm(uv[:, b, SG:2 * SG], uv[:, b, SG:2 * SG], sg_ln[:, l, 0, :], sg_ln[:, l, 1, :],
                               SG, sgv_ready)
                dve.wait_ge(used, l * LAYER_UNITS + 3)
                rotary_products(l, 0)
                dve.wait_ge(convT_pe, l + 1)
                for b in range(TB):
                    layer_norm(bank[7][:, b * CV:(b + 1) * CV], mix[:, b, ATT + SG:D], cv_ln[:, l, 0, :],
                               cv_ln[:, l, 1, :], CV, conv_ln_done)
                dve.wait_ge(spatial_pe, l + 1)
                for b in range(TB):
                    for g in range(GROUPS):
                        ins = dve.scalar_tensor_tensor(
                            out=mix[:, b, ATT + g * HD:ATT + (g + 1) * HD],
                            in0=bank[6][:, b * SG + g * HD:b * SG + (g + 1) * HD],
                            scalar=sgbT[:, l * GROUPS + g:l * GROUPS + g + 1],
                            in1=uv[:, b, g * HD:(g + 1) * HD], op0=ALU.add, op1=ALU.mult)
                ins.then_inc(sg_out, 1)
                dve.wait_ge(used, l * LAYER_UNITS + 4)
                rotary_products(l, 1)
                for b in range(TB):
                    dve.wait_ge(qkT_pe, 4 * l + 2 * b + 2)
                    dve.tensor_copy(qkT[:, 1, :, b * P:(b + 1) * P],
                                    bank[2 + b][:, :].rearrange("p (c t) -> p c t", c=4)).then_inc(qkT_dve, 1)
                for qb in range(TB):
                    for i in range((2, 4)[qb]):
                        dve.wait_ge(scores_pe, 6 * l + 2 * qb + i + 1)
                        if qb == 0:
                            src = bank[4 + i][:, :].rearrange("p (h k) -> p h k", h=4)
                            dst = row_max[:, 0, i::2]
                        else:
                            src = bank[i][:, :].rearrange("p (h k) -> p h k", h=2)
                            dst = row_max[:, 1, 4 * (i // 2) + i % 2:4 * (i // 2) + i % 2 + 3:2]
                        ins = dve.tensor_reduce(dst, src, AX_X, ALU.max)
                    step(ins)
                    dve.tensor_scalar(neg_max[:, qb, :], row_max[:, qb, :], -SCALE, None, ALU.mult).then_inc(max_ready, 1)
                for g in range(6):
                    dve.wait_ge(probT_pe, 6 * l + g + 1)
                    dve.tensor_copy(probT[:, g, :], bank[(g + 4) if g < 2 else g - 2][:, :]).then_inc(probT_ready, 1)
                step(dve.reciprocal(row_inv[:, :, :], row_sum[:, :, :]))
                for qb in range(TB):
                    dve.wait_ge(pv_pe, TB * l + qb + 1)
                    dve.tensor_tensor(mix[:, qb, 0:ATT].rearrange("p (h d) -> p h d", h=HEADS),
                                      bank[6 + qb][:, :].rearrange("p (h d) -> p h d", h=HEADS),
                                      row_inv[:, qb, :].unsqueeze(2).to_broadcast([P, HEADS, HD]), ALU.mult)\
                       .then_inc(att_out, 1)
                copy_columns(3 * l + 1)
                dve.wait_ge(used, l * LAYER_UNITS + 7)
                dve.wait_ge(par_in, 32 * (2 * l + 2))
                for b in range(TB):
                    for n in range(2):
                        ins = dve.scalar_tensor_tensor(out=h[:, b, n * BANK:(n + 1) * BANK],
                                                       in0=h[:, b, n * BANK:(n + 1) * BANK], scalar=ALPHA,
                                                       in1=bank[4 + 2 * b + n][:, :], op0=ALU.mult, op1=ALU.add)
                    step(ins)
                    layer_norm(h[:, b, :], h[:, b, :], ln_par[:, 0, :], ln_par[:, 1, :], D, h_ready)
                copy_columns(3 * l + 2)
                routing(l)
                dve.wait_ge(acc_init, TB * (l + 1))
                main, more = passes[l]
                with dve.Fori(0, ITERS) as it:
                    experts(l, main, 0, it)
                n = dve.value_load(fullest[0:1, l:l + 1], min_val=0, max_val=SEQ)
                with dve.If(n > SLOTS):
                    with dve.Fori(0, ROUNDS - 1) as rnd:
                        dve.tensor_scalar(slot[:, :, :, :], slot[:, :, :, :], -float(SLOTS), None, ALU.add)\
                           .then_inc(more.s["renumber"], 1)
                        with dve.Fori(0, ITERS) as it:
                            experts(l, more, rnd, it)
                dve.wait_ge(par_in, 32 * (2 * l + 3))
                for b in range(TB):
                    layer_norm(acc[:, b, :], h[:, b, :], ln_par[:, 0, :], ln_par[:, 1, :], D, h_ready)


_ORDER = ["x", "ln_in_g", "ln_in_b", "w_in", "w_out", "sg_ln_g", "sg_ln_b", "sg_w", "sg_b", "conv_w", "conv_b",
          "conv_ln_g", "conv_ln_b", "ln_mix_g", "ln_mix_b", "w_router", "router_bias", "w_gate", "w_up", "w_down",
          "ln_ffn_g", "ln_ffn_b"]


def kernel(**inputs):
    import concourse.bacc as bacc
    from concourse.bass_utils import run_bass_kernel_spmd

    nc = bacc.Bacc("TRN2", target_bir_lowering=False, num_devices=1)
    arrays, args = {}, []
    for name in _ORDER:
        a = np.ascontiguousarray(inputs[name])
        arrays[f"in_{name}"] = a
        args.append(nc.dram_tensor(f"in_{name}", a.shape, mybir.dt.from_np(a.dtype), kind="ExternalInput").ap())
    arrays["in_table"] = constants()
    args.append(nc.dram_tensor("in_table", (P, T_COLS), F32, kind="ExternalInput").ap())
    args.append(nc.dram_tensor("out_0", (1, SEQ, D), F32, kind="ExternalOutput").ap())
    trunk(nc, *args)
    r = run_bass_kernel_spmd(nc, [arrays], core_ids=[0])
    return r.results[0]["out_0"]
```

```python
import math
from contextlib import ExitStack

import numpy as np

import concourse.bass as bass
from concourse import mybir

ALU = mybir.AluOpType
ACT = mybir.ActivationFunctionType
AX_X = mybir.AxisListType.X
F32 = mybir.dt.float32
BF16 = mybir.dt.bfloat16
I32 = mybir.dt.int32

P = 128
SEQ = 256
TB = SEQ // P
D = 1024
KC = D // P
DEPTH = 2
HD = 64
HEADS = 8
ATT = HEADS * HD
SG = 256
GROUPS = 4
CV = 256
CB = CV // P
TAPS = 31
PAD = TAPS - 1
EXPERTS = 16
EGROUPS = 4
PER_GROUP = EXPERTS // EGROUPS
DE = 512
FC = DE // P
PAIRS = EXPERTS // 2
SLOTS = 64
ROUNDS = SEQ // SLOTS
EPS = 1e-5
NEG = -1e30
ALPHA = (2.0 * DEPTH) ** 0.25
SCALE = HD ** -0.5
BANK = 512

UNIT = 4096
RING = 8
SLABS = 5 + 2
PAIR_UNITS = 6
LAYER_UNITS = SLABS + PAIR_UNITS * PAIRS
SLAB_COLS = [2048, 0, 512, 1536, 1024]
BODY = 4
TURNS = BODY * PAIR_UNITS // RING
ITERS = PAIRS // BODY
assert BODY * PAIR_UNITS % RING == 0

T_COS, T_SIN, T_IOTA, T_TIE, T_FOLD, T_ID, T_BEFORE, T_MASK = 0, 64, 128, 192, 208, 224, 352, 480
T_COLS = T_MASK + 256
LN_TILES = 4 * TB
ZERO_COLS = 512


def constants():
    t = np.zeros((P, T_COLS), np.float32)
    half = HD // 2
    inv = (10000.0 ** (-np.arange(half, dtype=np.float64) / half)).astype(np.float32)
    ang = np.arange(SEQ, dtype=np.float32)[:, None] * inv[None, :]
    for b in range(TB):
        t[:, T_COS + b * half:T_COS + (b + 1) * half] = np.cos(ang[b * P:(b + 1) * P].astype(np.float64))
        t[:, T_SIN + b * half:T_SIN + (b + 1) * half] = np.sin(ang[b * P:(b + 1) * P].astype(np.float64))
    t[:, T_IOTA:T_IOTA + SLOTS] = np.arange(SLOTS)
    t[:, T_TIE:T_TIE + 16] = (np.arange(4)[None, :] < np.arange(4)[:, None]).reshape(-1)
    r = np.arange(P)
    t[:, T_ID:T_ID + P] = r[:, None] == r[None, :]
    t[:, T_FOLD:T_FOLD + EXPERTS] = r[:, None] % 32 == np.arange(EXPERTS)[None, :]
    t[:, T_BEFORE:T_BEFORE + P] = r[:, None] < r[None, :]
    t[:, T_MASK + P:T_MASK + 2 * P] = np.where(r[None, :] > r[:, None], np.float32(NEG), np.float32(0))
    return t


def trunk(nc, x, ln_in_g, ln_in_b, w_in, w_out, sg_ln_g, sg_ln_b, sg_w, sg_b, conv_w, conv_b,
          conv_ln_g, conv_ln_b, ln_mix_g, ln_mix_b, w_router, router_bias, w_gate, w_up, w_down,
          ln_ffn_g, ln_ffn_b, table, out):
    with ExitStack() as ctx:
        def sb(name, shape, dt=F32):
            return ctx.enter_context(nc.sbuf_tensor(name, [P] + shape, dt))

        def sem(name):
            return ctx.enter_context(nc.semaphore(name))

        bank = [ctx.enter_context(nc.psum_tensor(f"bank{i}", [P, BANK], F32)) for i in range(8)]

        ring = sb("ring", [RING, UNIT])
        h = sb("h", [TB, D])
        xT = sb("xT", [KC, SEQ])
        mix = sb("mix", [TB, D])
        acc = mix
        area_a = sb("area_a", [3072])
        area_b = sb("area_b", [3072])
        uv = sb("uv", [TB, 2 * SG])
        v_rows = mix[:, :, 0:ATT]
        glu = sb("glu", [CB, PAD + SEQ])
        conv = mix[:, 0, 0:CB * SEQ].rearrange("p (c t) -> p c t", c=CB)
        ln_par = sb("ln_par", [2, D])
        sg_ln = sb("sg_ln", [DEPTH, 2, SG])
        cv_ln = sb("cv_ln", [DEPTH, 2, CV])
        sgwT = sb("sgwT", [DEPTH, GROUPS, P])
        sgbT = sb("sgbT", [DEPTH * GROUPS])
        tapsT = sb("tapsT", [CB, DEPTH * TAPS + DEPTH])
        w_rt = sb("w_rt", [KC, 32])
        r_bias = sb("r_bias", [EXPERTS])
        tab = sb("tab", [T_BEFORE])
        before_bf = sb("before_bf", [P], BF16)
        ones_bf = sb("ones_bf", [P], BF16)
        ident_bf = sb("ident_bf", [P], BF16)
        mask_bf = sb("mask_bf", [2 * P], BF16)
        half_neg = sb("half_neg", [1])
        stats = sb("stats", [TB, 2, 6])
        mv = sb("mv", [TB, 2])
        n_ln = TB + DEPTH * LN_TILES
        var_eps = sb("var_eps", [n_ln])
        rstd = sb("rstd", [n_ln])
        row_max = sb("row_max", [TB, HEADS])
        neg_max = sb("neg_max", [TB, HEADS])
        row_sum = sb("row_sum", [TB, HEADS])
        row_inv = sb("row_inv", [TB, HEADS])
        gsum = sb("gsum", [3, TB * EGROUPS])
        mask_row = sb("mask_row", [TB, EXPERTS], BF16)
        wsum = sb("wsum", [2, TB])
        count = sb("count", [1])
        fullest = sb("fullest", [DEPTH], I32)
        slot = sb("slot", [PAIRS, TB, 2])
        gate = sb("gate", [PAIRS, TB, 2])

        qk_rows = area_a[:, 0:2048].rearrange("p (b n) -> p b n", b=TB)
        prob0 = area_a[:, 0:1024].rearrange("p (h k) -> p h k", h=HEADS)
        prob1 = area_a[:, 1024:3072].rearrange("p (h k) -> p h k", h=HEADS)
        conv_sig = area_a[:, 2048:2560].rearrange("p (c t) -> p c t", c=CB)
        by_cos = [area_b[:, i * 1024:i * 1024 + 512] for i in range(2)]
        by_sin = [area_b[:, i * 1024 + 512:i * 1024 + 1024] for i in range(2)]
        qkT = area_b[:, 0:2048].rearrange("p (i c t) -> p i c t", i=2, c=HEADS // 2)
        probT = area_b[:, :].rearrange("p (g n) -> p g n", g=6)
        xe = area_a[:, 0:1024].rearrange("p (c s) -> p c s", c=KC)
        silu = area_a[:, 1024:1536]
        hid = area_a[:, 1536:2048]
        hidT = area_a[:, 2048:2560].rearrange("p (c s) -> p c s", c=FC)
        y = area_b[:, 0:1024]
        back = [area_b[:, 1024 + 256 * i:1280 + 256 * i].rearrange("p (b t) -> p b t", b=TB) for i in range(2)]
        pick = area_b[:, 1536:1792].rearrange("p (b s) -> p b s", b=TB)
        pick_w = area_b[:, 1792:2048].rearrange("p (b s) -> p b s", b=TB)
        parts = area_b[:, 0:SEQ]
        sgw_rows = area_a[:, 0:1024].rearrange("p (n s) -> p n s", n=DEPTH * GROUPS)
        taps_rows = area_a[0:DEPTH * TAPS + DEPTH, 1024:1280]
        sgb_rows = area_a[0:DEPTH * GROUPS, 1280:1408]
        orders = area_b[:, 0:3 * P]
        cmp = area_b[:, 2048:2048 + 2 * TB * EXPERTS * PER_GROUP].rearrange("p (i n) -> p i n", i=2)
        rt_e, score, biased, rank, sel = (
            area_b[:, 2304 + 32 * i:2336 + 32 * i].rearrange("p (b e) -> p b e", b=TB) for i in range(5))

        ident = tab[:, T_ID:T_ID + P]
        fold = tab[:, T_FOLD:T_FOLD + EXPERTS]
        iota = tab[:, T_IOTA:T_IOTA + SLOTS]
        tie = tab[:, T_TIE:T_TIE + 16].rearrange("p (i j) -> p i j", i=4)

        x_in = sem("x_in")
        table_in = sem("table_in")
        setup_in = sem("setup_in")
        small_in = sem("small_in")
        par_in = sem("par_in")
        out_done = sem("out_done")
        landed = [sem(f"landed{i}") for i in range(RING)]
        used = sem("used")
        casts = sem("casts")
        pool_const = sem("pool_const")
        sgw_masked = sem("sgw_masked")
        setup_pe = sem("setup_pe")
        setup_copied = sem("setup_copied")
        h_ready = sem("h_ready")
        ln_var = sem("ln_var")
        ln_rstd = sem("ln_rstd")
        tr_pe = sem("tr_pe")
        tr_act = sem("tr_act")
        tr_dve = sem("tr_dve")
        sig_ready = sem("sig_ready")
        gelu_ready = sem("gelu_ready")
        sgv_ready = sem("sgv_ready")
        conv_step = sem("conv_step")
        glu_ready = sem("glu_ready")
        convT_pe = sem("convT_pe")
        spatial_pe = sem("spatial_pe")
        conv_ln_done = sem("conv_ln_done")
        conv_out = sem("conv_out")
        sg_out = sem("sg_out")
        rot_products = sem("rot_products")
        rot_done = sem("rot_done")
        v0_pe = sem("v0_pe")
        v_ready = sem("v_ready")
        qkT_pe = sem("qkT_pe")
        qkT_act = sem("qkT_act")
        qkT_dve = sem("qkT_dve")
        scores_pe = sem("scores_pe")
        max_ready = sem("max_ready")
        exp_done = sem("exp_done")
        probT_pe = sem("probT_pe")
        probT_ready = sem("probT_ready")
        pv_pe = sem("pv_pe")
        att_out = sem("att_out")
        proj_pe = sem("proj_pe")
        parts_pe = sem("parts_pe")
        parts_copied = sem("parts_copied")
        router_pe = sem("router_pe")
        router_exp = sem("router_exp")
        mask_ready = sem("mask_ready")
        before_pe = sem("before_pe")
        routed = sem("routed")
        acc_init = sem("acc_init")
        dve_step = sem("dve_step")

        class Pass:

            def __init__(self, name, used_sem, landed_sems, unit0, used0, pair0, rounds):
                self.unit0 = unit0
                self.load0 = unit0 if rounds == 1 and name == "main" else 0
                self.used0 = used0
                self.pair0 = pair0
                self.rounds = rounds
                self.used = used_sem
                self.landed = landed_sems

        def moe_sems(name):
            return {k: sem(f"{name}_{k}") for k in (
                "pick", "gathered", "pick_t", "xe", "back", "silu", "hid", "hid_t", "hidT", "y", "comb", "added", "renumber")}

        main_sems = moe_sems("moe")
        passes = []
        for l in range(DEPTH):
            m = Pass("main", used, landed, l * LAYER_UNITS + SLABS, l * LAYER_UNITS + SLABS, l * PAIRS, 1)
            m.s = main_sems
            more_used = sem(f"more{l}_used")
            more_landed = [sem(f"more{l}_landed{i}") for i in range(RING)]
            o = Pass("more", more_used, more_landed, l * LAYER_UNITS + SLABS, RING, 0, ROUNDS - 1)
            o.s = moe_sems(f"more{l}")
            passes.append((m, o))

        def unit_at(n):
            return ring[:, n % RING, :]

        def wait_unit(pe, n):
            pe.wait_ge(landed[n % RING], 16 * (n // RING + 1))

        def bcast_row(ap1d, n):
            return ap1d.rearrange("(a n) -> a n", a=1).to_broadcast([P, n])

        block = ctx.enter_context(nc.Block())

        @block.sync
        def _(sp):
            for b in range(TB):
                sp.dma_start(h[:, b, :], x[0, b * P:(b + 1) * P, :]).then_inc(x_in, 16)
            sp.dma_start(tab[:, :], table[:, 0:T_BEFORE]).then_inc(table_in, 16)
            sp.dma_start(ln_par[:, 0, :], bcast_row(ln_in_g, D)).then_inc(par_in, 16)
            sp.dma_start(ln_par[:, 1, :], bcast_row(ln_in_b, D)).then_inc(par_in, 16)

            def load_setup():
                sp.dma_start(taps_rows[0:DEPTH * TAPS, :], conv_w.rearrange("l k c -> (l k) c")).then_inc(setup_in, 16)
                sp.dma_start(taps_rows[DEPTH * TAPS:, :], conv_b).then_inc(setup_in, 16)
                sp.dma_start(sgb_rows, sg_b.rearrange("l g t -> (l g) t")).then_inc(setup_in, 16)
                sp.dma_start(sgw_rows, sg_w.rearrange("l g t s -> t (l g) s")).then_inc(setup_in, 16)

            def load_small():
                sp.dma_start(orders, table[:, T_BEFORE:T_COLS]).then_inc(small_in, 16)
                sp.wait_ge(pool_const, 4)
                sp.dma_start(w_rt[:, :, 0:EXPERTS], w_router.rearrange("(p c) n -> p c n", c=KC)).then_inc(small_in, 16)
                sp.dma_start(r_bias[:, :], bcast_row(router_bias, EXPERTS)).then_inc(small_in, 16)
                for dst, g, s in ((sg_ln, sg_ln_g, sg_ln_b), (cv_ln, conv_ln_g, conv_ln_b)):
                    for i, src in enumerate((g, s)):
                        sp.dma_start(dst[:, :, i, :],
                                     src.rearrange("(a l) n -> a l n", a=1).to_broadcast([P, DEPTH, SG]))\
                          .then_inc(small_in, 16)

            def load_slab(l, i, n):
                if n >= RING:
                    sp.wait_ge(used, n - RING + 1)
                dst = unit_at(n).rearrange("p (c n) -> p c n", c=KC)
                if i < 5:
                    src = w_in[l].rearrange("(p c) n -> p c n", c=KC)[:, :, SLAB_COLS[i]:SLAB_COLS[i] + BANK]
                else:
                    src = w_out[l].rearrange("(p c) n -> p c n", c=KC)[:, :, (i - 5) * BANK:(i - 4) * BANK]
                sp.dma_start(dst, src).then_inc(landed[n % RING], 16)

            def load_pairs(l, ps, rnd, it):
                for j in range(BODY):
                    first = it * (2 * BODY) + 2 * j
                    for u in range(PAIR_UNITS):
                        k = PAIR_UNITS * j + u
                        turn = rnd * (ITERS * BODY * PAIR_UNITS) + it * (BODY * PAIR_UNITS)
                        sp.wait_ge(ps.used, turn + (ps.used0 + k - RING + 1))
                        half = u // 2 if u < 4 else u - 4
                        if u < 4:
                            w = (w_gate, w_up)[u % 2][l].rearrange("e (p c) n -> p e (c n)", c=KC)
                        else:
                            w = w_down[l].rearrange("e (p c) n -> p e (c n)", c=FC)
                        src = w[:, bass.ds(first, 2), half * 2048:(half + 1) * 2048]
                        at = (ps.unit0 + k) % RING
                        sp.dma_start(ring[:, at, :].rearrange("p (e n) -> p e n", e=2), src)\
                          .then_inc(ps.landed[at], 16)

            for l in range(DEPTH):
                main, more = passes[l]
                for i in range(SLABS):
                    load_slab(l, i, l * LAYER_UNITS + i)
                    if l == 0 and i == 0:
                        load_setup()
                    if l == 0 and i == 1:
                        load_small()
                with sp.Fori(0, ITERS) as it:
                    load_pairs(l, main, 0, it)
                sp.wait_ge(routed, l + 1)
                n = sp.value_load(fullest[0:1, l:l + 1], min_val=0, max_val=SEQ)
                with sp.If(n > SLOTS):
                    sp.wait_ge(used, (l + 1) * LAYER_UNITS)
                    sp.sem_inc(more.used, RING)
                    with sp.Fori(0, ROUNDS - 1) as rnd:
                        with sp.Fori(0, ITERS) as it:
                            load_pairs(l, more, rnd, it)
                    sp.wait_ge(more.used, RING + (ROUNDS - 1) * PAIRS * PAIR_UNITS)
            for b in range(TB):
                sp.wait_ge(h_ready, 2 * TB * DEPTH + b + 1)
                sp.dma_start(out[0, b * P:(b + 1) * P, :], h[:, b, :]).then_inc(out_done, 16)
            sp.wait_ge(out_done, 16 * TB)

        @block.tensor
        def _(pe):
            pe.wait_ge(table_in, 16)

            def setup():
                pe.wait_ge(setup_in, 16 * 4)
                pe.wait_ge(sgw_masked, 1)
                nt = DEPTH * TAPS + DEPTH
                for cb in range(CB):
                    pe.transpose(bank[3][:, cb * nt:(cb + 1) * nt], taps_rows[:, cb * P:(cb + 1) * P],
                                 ident[0:nt, 0:nt])
                pe.transpose(bank[3][:, 256:256 + DEPTH * GROUPS], sgb_rows,
                             ident[0:DEPTH * GROUPS, 0:DEPTH * GROUPS]).then_inc(setup_pe, 1)
                for n in range(DEPTH * GROUPS):
                    mm = pe.transpose(bank[6 + n // 4][:, (n % 4) * P:(n % 4 + 1) * P], sgw_rows[:, n, :], ident)
                    if n % 4 == 3:
                        mm.then_inc(setup_pe, 1)

            def turn(src, b, stage):
                for half in range(2):
                    dst = bank[2 * b + half]
                    for c in range(4):
                        mm = pe.transpose(dst[:, c * P:(c + 1) * P], src[:, b, 4 * half + c::KC], ident)
                    mm.then_inc(tr_pe, 1)

            def wait_xT(stage):
                pe.wait_ge(tr_act, 2 * (stage + 1))
                pe.wait_ge(tr_dve, 2 * (stage + 1))

            def block_slab(n, b, dst):
                wait_unit(pe, n)
                w = unit_at(n).rearrange("p (c n) -> p c n", c=KC)
                for c in range(KC):
                    mm = pe.matmul(dst[:, :], xT[:, c, b * P:(b + 1) * P], w[:, c, :],
                                   start=c == 0, stop=c == KC - 1)
                if b == TB - 1:
                    mm.then_inc(used, 1)
                return mm

            def rows_slab(n, banks):
                for b in range(TB):
                    block_slab(n, b, bank[banks[b]])

            def experts(l, ps, rnd, it):
                s = ps.s
                pairs_before = rnd * PAIRS + it * BODY

                def nth(name, j, k=1, per=1):
                    pe.wait_ge(s[name], pairs_before * per + ((ps.pair0 + j) * per + k))

                def landed_unit(k):
                    at = (ps.unit0 + k) % RING
                    turns = rnd * (ITERS * TURNS * 16) + it * (TURNS * 16)
                    pe.wait_ge(ps.landed[at], turns + 16 * ((ps.load0 + k) // RING + 1))
                    return ring[:, at, :]

                def gather(j):
                    nth("pick", j, 1, 2)
                    for c in range(KC):
                        for b in range(TB):
                            mm = pe.matmul(bank[c // 4][:, (c % 4) * P:(c % 4 + 1) * P], h[:, b, c::KC],
                                           pick[:, b, :], start=b == 0, stop=b == TB - 1)
                        if c % 4 == 3:
                            mm.then_inc(s["gathered"], 1)
                    nth("pick", j, 2, 2)
                    if j >= 2:
                        nth("added", j - 2, 3, 4)
                    elif j == 1:
                        nth("back", 0)
                    for b in range(TB):
                        mm = pe.transpose(bank[7][:, b * P:(b + 1) * P], pick_w[:, b, :], ident)
                    mm.then_inc(s["pick_t"], 1)

                def gate_up(j):
                    nth("xe", j, 2, 2)
                    for u in range(4):
                        w = landed_unit(PAIR_UNITS * j + u).rearrange("p (e c n) -> p e c n", e=2, c=4)
                        for c in range(4):
                            for e in range(2):
                                k = 4 * (u // 2) + c
                                mm = pe.matmul(bank[2 + u % 2][e * SLOTS:(e + 1) * SLOTS, :],
                                               xe[:, k, e * SLOTS:(e + 1) * SLOTS], w[:, e, c, :],
                                               start=k == 0, stop=k == KC - 1)
                        mm.then_inc(ps.used, 1)

                def turn_hid(j):
                    nth("hid", j)
                    if j >= 1:
                        nth("added", j - 1, 4, 4)
                    for c in range(FC):
                        mm = pe.transpose(bank[4][:, c * P:(c + 1) * P], hid[:, c::FC], ident)
                    mm.then_inc(s["hid_t"], 1)

                def down(j):
                    nth("hidT", j)
                    for u in range(2):
                        w = landed_unit(PAIR_UNITS * j + 4 + u).rearrange("p (e c n) -> p e c n", e=2, c=2)
                        for n in range(2):
                            for c in range(2):
                                for e in range(2):
                                    k = 2 * u + c
                                    mm = pe.matmul(bank[5 + n][e * SLOTS:(e + 1) * SLOTS, :],
                                                   hidT[:, k, e * SLOTS:(e + 1) * SLOTS],
                                                   w[:, e, c, n * BANK:(n + 1) * BANK],
                                                   start=k == 0, stop=k == FC - 1)
                        mm.then_inc(ps.used, 1)

                def combine(j):
                    nth("y", j, 2, 2)
                    nth("back", min(j + 1, BODY - 1))
                    for k in range(4):
                        b, n = k // 2, k % 2
                        if k >= 2:
                            nth("added", j, k - 1, 4)
                        mm = pe.matmul(bank[(7, 4)[k % 2]][:, :], back[j % 2][:, b, :],
                                       y[:, n * BANK:(n + 1) * BANK], start=True, stop=True)
                        mm.then_inc(s["comb"], 1)

                gather(0)
                for j in range(BODY):
                    gate_up(j)
                    if j:
                        combine(j - 1)
                    if j < BODY - 1:
                        gather(j + 1)
                    turn_hid(j)
                    down(j)
                combine(BODY - 1)
                nth("added", BODY - 1, 4, 4)

            for l in range(DEPTH):
                u0 = l * LAYER_UNITS
                for b in range(TB):
                    pe.wait_ge(h_ready, 2 * TB * l + b + 1)
                    turn(h, b, 3 * l)
                wait_xT(3 * l)
                wait_unit(pe, u0)
                w = unit_at(u0).rearrange("p (c n) -> p c n", c=KC)
                for k in (2, 3, 0, 1):
                    for c in range(KC):
                        mm = pe.matmul(bank[4 + k // 2][:, (k % 2) * SEQ:(k % 2 + 1) * SEQ],
                                       w[:, c, k * P:(k + 1) * P], xT[:, c, :], start=c == 0, stop=c == KC - 1)
                mm.then_inc(used, 1)
                if l == 0:
                    setup()
                rows_slab(u0 + 1, (0, 1))
                if l == 0:
                    pe.wait_ge(setup_copied, 1)
                rows_slab(u0 + 2, (2, 3))
                pe.wait_ge(conv_step, CB * TAPS * (l + 1))
                for b in range(TB):
                    for cb in range(CB):
                        mm = pe.transpose(bank[4][:, b * CV + cb * P:b * CV + (cb + 1) * P],
                                          conv[:, cb, b * P:(b + 1) * P], ident)
                mm.then_inc(convT_pe, 1)
                rows_slab(u0 + 3, (6, 7))
                pe.wait_ge(rot_done, 2 * TB * (l + 1))
                for b in range(TB):
                    for i in range(2):
                        for hp in range(HEADS // 2):
                            mm = pe.transpose(bank[2 * i + b][:, hp * P:(hp + 1) * P],
                                              qk_rows[:, b, i * ATT + hp * P:i * ATT + (hp + 1) * P], ident)
                        mm.then_inc(qkT_pe, 1)
                pe.wait_ge(conv_ln_done, TB * (l + 1))
                block_slab(u0 + 4, 0, bank[4]).then_inc(v0_pe, 1)
                pe.wait_ge(gelu_ready, TB * (l + 1))
                pe.wait_ge(qkT_act, 2 * l + 1)
                pe.wait_ge(qkT_dve, 2 * l + 1)
                for par in range(2):
                    pe.matmul(bank[6 + par][:, :], ident_bf[:, :],
                              mask_bf[:, P:2 * P].unsqueeze(1).to_broadcast([P, 4, P]), start=True, stop=False,
                              skip_group_check=True)
                for hp in range(HEADS // 2):
                    for par in range(2):
                        q = slice(par * HD, (par + 1) * HD)
                        mm = pe.matmul(bank[6 + par][:, hp * P:(hp + 1) * P], qkT[q, 0, hp, 0:P], qkT[q, 1, hp, 0:P],
                                       start=False, stop=True, skip_group_check=True)
                        if hp == HEADS // 2 - 1:
                            mm.then_inc(scores_pe, 1)
                pe.wait_ge(qkT_act, 2 * (l + 1))
                pe.wait_ge(qkT_dve, 2 * (l + 1))
                for i in range(4):
                    pe.matmul(bank[i][:, :], ident_bf[:, :],
                              mask_bf[:, :].unsqueeze(1).to_broadcast([P, 2, 2 * P]), start=True, stop=False,
                              skip_group_check=True)
                for hp in range(HEADS // 2):
                    for par in range(2):
                        q = slice(par * HD, (par + 1) * HD)
                        mm = pe.matmul(bank[2 * (hp // 2) + par][:, (hp % 2) * SEQ:(hp % 2 + 1) * SEQ],
                                       qkT[q, 0, hp, P:2 * P], qkT[q, 1, hp, :],
                                       start=False, stop=True, skip_group_check=True)
                        if hp % 2 == 1:
                            mm.then_inc(scores_pe, 1)
                block_slab(u0 + 4, 1, bank[5])
                pe.wait_ge(v_ready, TB * l + 1)
                for b in range(TB):
                    pe.wait_ge(sgv_ready, TB * l + b + 1)
                    for g in range(GROUPS):
                        mm = pe.matmul(bank[4][:, b * SG + g * HD:b * SG + (g + 1) * HD], sgwT[:, l, g, :],
                                       uv[:, b, SG + g * HD:SG + (g + 1) * HD], start=True, stop=True)
                mm.then_inc(spatial_pe, 1)
                pe.wait_ge(exp_done, 2 * HEADS * l + HEADS)
                for g in range(2):
                    for i in range(4):
                        mm = pe.transpose(bank[6 + g][:, i * P:(i + 1) * P], prob0[:, 4 * g + i, :], ident)
                    mm.then_inc(probT_pe, 1)
                for g in range(4):
                    pe.wait_ge(exp_done, 2 * HEADS * l + HEADS + 4 * (g // 2 + 1))
                    for i in range(4):
                        mm = pe.transpose(bank[g][:, i * P:(i + 1) * P],
                                          prob1[:, 2 * g + i // 2, (i % 2) * P:(i % 2 + 1) * P], ident)
                    mm.then_inc(probT_pe, 1)
                pe.wait_ge(sg_out, l + 1)
                pe.wait_ge(v_ready, TB * (l + 1))
                for hd in range(HEADS):
                    if hd % 4 == 0:
                        pe.wait_ge(probT_ready, 6 * l + hd // 4 + 1)
                    mm = pe.matmul(bank[4][:, hd * HD:(hd + 1) * HD], probT[:, hd // 4, (hd % 4) * P:(hd % 4 + 1) * P],
                                   v_rows[:, 0, hd * HD:(hd + 1) * HD], start=True, stop=True)
                mm.then_inc(pv_pe, 1)
                for hd in range(HEADS):
                    if hd % 2 == 0:
                        pe.wait_ge(probT_ready, 6 * l + 2 + hd // 2 + 1)
                    for kb in range(TB):
                        i = 2 * (hd % 2) + kb
                        mm = pe.matmul(bank[5][:, hd * HD:(hd + 1) * HD], probT[:, 2 + hd // 2, i * P:(i + 1) * P],
                                       v_rows[:, kb, hd * HD:(hd + 1) * HD], start=kb == 0, stop=kb == 1)
                mm.then_inc(pv_pe, 1)
                pe.wait_ge(conv_out, l + 1)
                for b in range(TB):
                    pe.wait_ge(att_out, TB * l + b + 1)
                    turn(mix, b, 3 * l + 1)
                wait_xT(3 * l + 1)
                for b in range(TB):
                    for n in range(2):
                        mm = block_slab(u0 + 5 + n, b, bank[4 + 2 * b + n])
                    if b == 0:
                        mm.then_inc(proj_pe, 1)
                for b in range(TB):
                    pe.wait_ge(h_ready, 2 * TB * l + TB + b + 1)
                    turn(h, b, 3 * l + 2)
                wait_xT(3 * l + 2)
                for c in range(KC):
                    g = slice(32 * (c % 4), 32 * (c % 4 + 1))
                    mm = pe.matmul(bank[6][g, 0:SEQ], w_rt[:, c, :], xT[:, c, :], start=c < 4, stop=c >= 4,
                                   tile_position=(0, 32 * (c % 4)))
                mm.then_inc(parts_pe, 1)
                pe.wait_ge(parts_copied, l + 1)
                for b in range(TB):
                    mm = pe.matmul(bank[4][:, b * EXPERTS:(b + 1) * EXPERTS], parts[:, b * P:(b + 1) * P], fold,
                                   start=True, stop=True)
                mm.then_inc(router_pe, 1)
                pe.wait_ge(mask_ready, l + 1)
                pe.wait_ge(casts, 3)
                pe.matmul(bank[5][:, 0:16], before_bf[:, :], mask_row[:, 0, :], start=True, stop=True)
                pe.matmul(bank[5][:, 16:32], ones_bf[:, :], mask_row[:, 0, :], start=True, stop=False)
                pe.matmul(bank[5][:, 16:32], before_bf[:, :], mask_row[:, 1, :], start=False, stop=True)
                pe.matmul(bank[5][:, 32:48], ones_bf[:, :], mask_row[:, 0, :], start=True, stop=False)
                pe.matmul(bank[5][:, 32:48], ones_bf[:, :], mask_row[:, 1, :], start=False, stop=True)\
                  .then_inc(before_pe, 1)
                main, more = passes[l]
                with pe.Fori(0, ITERS) as it:
                    experts(l, main, 0, it)
                pe.wait_ge(routed, l + 1)
                n = pe.value_load(fullest[0:1, l:l + 1], min_val=0, max_val=SEQ)
                with pe.If(n > SLOTS):
                    with pe.Fori(0, ROUNDS - 1) as rnd:
                        with pe.Fori(0, ITERS) as it:
                            experts(l, more, rnd, it)

        @block.scalar
        def _(act):
            def next_params(n, gain, shift, free_after):
                act.wait_ge(h_ready, free_after)
                act.dma_start(ln_par[:, 0, :], bcast_row(gain, D)).then_inc(par_in, 16)
                act.dma_start(ln_par[:, 1, :], bcast_row(shift, D)).then_inc(par_in, 16)

            def copy_columns(stage):
                for b in range(TB):
                    act.wait_ge(tr_pe, 4 * stage + 2 * b + 1)
                    act.activation(xT[:, 0:4, b * P:(b + 1) * P],
                                   bank[2 * b][:, :].rearrange("p (c t) -> p c t", c=4), ACT.Copy).then_inc(tr_act, 1)

            def experts(l, ps, rnd, it):
                s = ps.s
                pairs_before = rnd * PAIRS + it * BODY
                units_before = pairs_before * PAIR_UNITS

                def nth(name, j, k=1, per=1):
                    act.wait_ge(s[name], pairs_before * per + ((ps.pair0 + j) * per + k))

                def tokens(j):
                    for half in range(2):
                        nth("gathered", j, half + 1, 2)
                        act.activation(xe[:, 4 * half:4 * half + 4, :],
                                       bank[half][:, :].rearrange("p (c s) -> p c s", c=4), ACT.Copy)\
                           .then_inc(s["xe"], 1)
                    nth("pick_t", j)
                    act.activation(back[j % 2], bank[7][:, 0:SEQ].rearrange("p (b t) -> p b t", b=TB), ACT.Copy)\
                       .then_inc(s["back"], 1)

                tokens(0)
                for j in range(BODY):
                    act.wait_ge(ps.used, units_before + (ps.used0 + PAIR_UNITS * j + 4))
                    act.activation(silu, bank[2][:, :], ACT.Silu).then_inc(s["silu"], 1)
                    if j < BODY - 1:
                        tokens(j + 1)
                    act.wait_ge(ps.used, units_before + (ps.used0 + PAIR_UNITS * (j + 1)))
                    for n in range(2):
                        act.activation(y[:, n * BANK:(n + 1) * BANK], bank[5 + n][:, :], ACT.Copy)\
                           .then_inc(s["y"], 1)

            for l in range(DEPTH):
                next_params(2 * l + 1, ln_mix_g[l], ln_mix_b[l], 2 * TB * l + TB)
                copy_columns(3 * l)
                act.wait_ge(used, l * LAYER_UNITS + 1)
                act.activation(conv_sig, bank[5][:, :].rearrange("p (c t) -> p c t", c=CB), ACT.Sigmoid)\
                   .then_inc(sig_ready, 1)
                act.wait_ge(conv_ln_done, TB * (l + 1))
                act.activation(mix[:, :, ATT + SG:D], mix[:, :, ATT + SG:D], ACT.Silu).then_inc(conv_out, 1)
                act.wait_ge(used, l * LAYER_UNITS + 4)
                for b in range(TB):
                    act.activation(uv[:, b, :], bank[6 + b][:, :], ACT.Gelu_apprx_tanh).then_inc(gelu_ready, 1)
                for b in range(TB):
                    act.wait_ge(qkT_pe, 4 * l + 2 * b + 1)
                    act.activation(qkT[:, 0, :, b * P:(b + 1) * P],
                                   bank[b][:, :].rearrange("p (c t) -> p c t", c=4), ACT.Copy).then_inc(qkT_act, 1)
                act.wait_ge(v0_pe, l + 1)
                act.activation(v_rows[:, 0, :], bank[4][:, :], ACT.Copy).then_inc(v_ready, 1)
                for qb in range(TB):
                    act.wait_ge(max_ready, TB * l + qb + 1)
                    for hd in range(HEADS):
                        if qb == 0:
                            src, dst = bank[6 + hd % 2][:, (hd // 2) * P:(hd // 2 + 1) * P], prob0[:, hd, :]
                        else:
                            src = bank[2 * (hd // 4) + hd % 2][:, (hd // 2 % 2) * SEQ:(hd // 2 % 2 + 1) * SEQ]
                            dst = prob1[:, hd, :]
                        act.activation(dst, src, ACT.Exp, bias=neg_max[:, qb, hd:hd + 1], scale=SCALE,
                                       accum_out=row_sum[:, qb, hd:hd + 1]).then_inc(exp_done, 1)
                act.wait_ge(used, l * LAYER_UNITS + 5)
                act.activation(v_rows[:, 1, :], bank[5][:, :], ACT.Copy).then_inc(v_ready, 1)
                copy_columns(3 * l + 1)
                copy_columns(3 * l + 2)
                next_params(2 * l + 2, ln_ffn_g[l], ln_ffn_b[l], 2 * TB * l + 2 * TB)
                act.wait_ge(parts_pe, l + 1)
                act.activation(parts, bank[6][:, 0:SEQ], ACT.Copy).then_inc(parts_copied, 1)
                act.wait_ge(router_pe, l + 1)
                act.activation(rt_e[:, :, :], bank[4][:, 0:TB * EXPERTS].rearrange("p (b e) -> p b e", b=TB),
                               ACT.Exp, scale=-1.0).then_inc(router_exp, 1)
                main, more = passes[l]
                with act.Fori(0, ITERS) as it:
                    experts(l, main, 0, it)
                act.wait_ge(routed, l + 1)
                n = act.value_load(fullest[0:1, l:l + 1], min_val=0, max_val=SEQ)
                with act.If(n > SLOTS):
                    with act.Fori(0, ROUNDS - 1) as rnd:
                        with act.Fori(0, ITERS) as it:
                            experts(l, more, rnd, it)

        @block.gpsimd
        def _(pool):
            norms = [0]

            def inverse_deviations(n):
                for _ in range(n):
                    i = norms[0]
                    norms[0] += 1
                    pool.wait_ge(ln_var, i + 1)
                    pool.tensor_tensor(rstd[:, i:i + 1], var_eps[:, i:i + 1], half_neg[:, :], ALU.pow)\
                        .then_inc(ln_rstd, 1)

            pool.memset(half_neg[:, :], -0.5).then_inc(pool_const, 1)
            pool.memset(ones_bf[:, :], 1.0).then_inc(pool_const, 1)
            pool.memset(glu[:, :, 0:PAD], 0.0).then_inc(pool_const, 1)
            pool.memset(w_rt[:, :, :], 0.0).then_inc(pool_const, 1)
            pool.wait_ge(pool_const, 4)
            inverse_deviations(TB)
            pool.wait_ge(setup_in, 16 * 4)
            pool.affine_select(out=sgw_rows, in_=sgw_rows, compare_op=ALU.is_ge, fill=0.0, base=0,
                               pattern=[[0, DEPTH * GROUPS], [-1, P]], channel_multiplier=1).then_inc(sgw_masked, 1)

            def rotate(l, i):
                for b in range(TB):
                    pool.wait_ge(rot_products, 2 * TB * l + 2 * i + b + 1)
                    a = by_cos[b].rearrange("p (h x d) -> p h x d", h=HEADS, x=2)
                    s = by_sin[b].rearrange("p (h x d) -> p h x d", h=HEADS, x=2)
                    o = qk_rows[:, b, i * ATT:(i + 1) * ATT].rearrange("p (h x d) -> p h x d", h=HEADS, x=2)
                    pool.tensor_tensor(o[:, :, 0, :], a[:, :, 0, :], s[:, :, 1, :], ALU.subtract)
                    pool.tensor_tensor(o[:, :, 1, :], a[:, :, 1, :], s[:, :, 0, :], ALU.add).then_inc(rot_done, 1)

            for l in range(DEPTH):
                rotate(l, 0)
                rotate(l, 1)
                inverse_deviations(TB)
                inverse_deviations(TB)
                inverse_deviations(TB)
                for b in range(TB):
                    pool.wait_ge(h_ready, 2 * TB * l + TB + b + 1)
                    pool.tensor_scalar(acc[:, b, :], h[:, b, :], ALPHA, 1.0, ALU.mult, ALU.mult).then_inc(acc_init, 1)
                inverse_deviations(TB)

        @block.vector
        def _(dve):
            steps = [0]

            def step(ins):
                steps[0] += 1
                ins.then_inc(dve_step, 1)
                dve.wait_ge(dve_step, steps[0])

            norms = [0]

            def norm_stats(src, b, width):
                i = norms[0]
                norms[0] += 1
                parts = max(1, width // BANK)
                w = width // parts
                for k in range(parts):
                    ins = dve.bn_stats(stats[:, b, k, :], src[:, k * w:(k + 1) * w])
                step(ins)
                step(dve.bn_aggr(mv[:, b, :], stats[:, b, 0:parts, :]))
                dve.tensor_scalar(var_eps[:, i:i + 1], mv[:, b, 1:2], EPS, None, ALU.add).then_inc(ln_var, 1)
                return i

            def norm_apply(i, src, dst, b, gain, shift, signal):
                step(dve.scalar_tensor_tensor(out=dst, in0=src, scalar=mv[:, b, 0:1], in1=gain,
                                              op0=ALU.subtract, op1=ALU.mult))
                dve.wait_ge(ln_rstd, i + 1)
                dve.scalar_tensor_tensor(out=dst, in0=dst, scalar=rstd[:, i:i + 1], in1=shift,
                                         op0=ALU.mult, op1=ALU.add).then_inc(signal, 1)

            def layer_norm(src, dst, b, gain, shift, width, signal):
                norm_apply(norm_stats(src, b, width), src, dst, b, gain, shift, signal)

            def layer_norms(src, dst, gain, shift, width, signal):
                i = [norm_stats(src(b), b, width) for b in range(TB)]
                for b in range(TB):
                    norm_apply(i[b], src(b), dst(b), b, gain, shift, signal)

            def copy_columns(stage):
                for b in range(TB):
                    dve.wait_ge(tr_pe, 4 * stage + 2 * b + 2)
                    dve.tensor_copy(xT[:, 4:8, b * P:(b + 1) * P],
                                    bank[2 * b + 1][:, :].rearrange("p (c t) -> p c t", c=4)).then_inc(tr_dve, 1)

            def rotary_products(l, i):
                for b in range(TB):
                    src = bank[2 * i + b][:, :].rearrange("p (h d) -> p h d", d=HD // 2)
                    if i == 1:
                        dve.wait_ge(rot_done, 2 * TB * l + b + 1)
                    for t0, dst in ((T_COS, by_cos[b]), (T_SIN, by_sin[b])):
                        angle = tab[:, t0 + b * 32:t0 + (b + 1) * 32].unsqueeze(1).to_broadcast([P, 16, 32])
                        ins = dve.tensor_tensor(dst.rearrange("p (h d) -> p h d", d=HD // 2), src, angle, ALU.mult)
                    ins.then_inc(rot_products, 1)

            def routing(l):
                sc = score[:, :, :].rearrange("p b e -> p (b e)")
                bi = biased[:, :, :].rearrange("p b e -> p (b e)")
                se = sel[:, :, :].rearrange("p b e -> p (b e)")
                ra = rank[:, :, :].rearrange("p b e -> p (b e)")
                ex = rt_e[:, :, :].rearrange("p b e -> p (b e)")
                dve.wait_ge(router_exp, l + 1)
                step(dve.tensor_scalar(ex, ex, 1.0, None, ALU.add))
                step(dve.reciprocal(sc, ex))
                step(dve.tensor_tensor(biased[:, :, :], score[:, :, :],
                                       r_bias[:, :].unsqueeze(1).to_broadcast([P, TB, EXPERTS]), ALU.add))

                def ranks(v, n, m, dst):
                    them = v.rearrange("p (g j) -> p g j", j=m).unsqueeze(2).to_broadcast([P, n, m, m])
                    one = v.rearrange("p (g j) -> p g j", j=m).unsqueeze(3).to_broadcast([P, n, m, m])
                    c0 = cmp[:, 0, 0:n * m * m].rearrange("p (g i j) -> p g i j", i=m, j=m)
                    c1 = cmp[:, 1, 0:n * m * m].rearrange("p (g i j) -> p g i j", i=m, j=m)
                    dve.tensor_tensor(c0, them, one, ALU.is_gt)
                    step(dve.tensor_tensor(c1, them, one, ALU.is_equal))
                    step(dve.tensor_tensor(c1, c1, tie.unsqueeze(1).to_broadcast([P, n, m, m]), ALU.mult))
                    step(dve.tensor_tensor(c0, c0, c1, ALU.add))
                    step(dve.tensor_reduce(dst, c0, AX_X, ALU.add))

                ranks(bi, TB * EGROUPS, PER_GROUP, ra.rearrange("p (g j) -> p g j", j=PER_GROUP))
                step(dve.tensor_scalar(se, ra, 2.0, None, ALU.is_lt))
                step(dve.tensor_tensor(ra, se, bi, ALU.mult))
                step(dve.tensor_reduce(gsum[:, 0, :], ra.rearrange("p (g j) -> p g j", j=PER_GROUP), AX_X, ALU.add))
                ranks(gsum[:, 0, :], TB, EGROUPS, gsum[:, 1, :].rearrange("p (g j) -> p g j", j=EGROUPS))
                step(dve.tensor_scalar(gsum[:, 2, :], gsum[:, 1, :], 1.0, None, ALU.is_lt))
                step(dve.tensor_tensor(se.rearrange("p (g j) -> p g j", j=PER_GROUP),
                                       se.rearrange("p (g j) -> p g j", j=PER_GROUP),
                                       gsum[:, 2, :].unsqueeze(2).to_broadcast([P, TB * EGROUPS, PER_GROUP]), ALU.mult))
                dve.tensor_copy(mask_row[:, :, :], sel[:, :, :]).then_inc(mask_ready, 1)
                step(dve.tensor_tensor(ra, se, sc, ALU.mult))
                step(dve.tensor_reduce(wsum[:, 0, :], rank[:, :, :], AX_X, ALU.add))
                step(dve.reciprocal(wsum[:, 1, :], wsum[:, 0, :]))
                for b in range(TB):
                    dve.tensor_scalar(gate[:, :, b, :], rank[:, b, :].rearrange("p (i e) -> p i e", e=2),
                                      wsum[:, 1, b:b + 1], None, ALU.mult)
                numbered = cmp[:, 0, 0:TB * EXPERTS].rearrange("p (b e) -> p b e", b=TB)
                dve.wait_ge(before_pe, l + 1)
                for b in range(TB):
                    ins = dve.scalar_tensor_tensor(out=numbered[:, b, :], in0=bank[5][:, b * 16:(b + 1) * 16], scalar=1.0,
                                                   in1=sel[:, b, :], op0=ALU.add, op1=ALU.mult)
                step(ins)
                for b in range(TB):
                    dve.tensor_scalar(slot[:, :, b, :], numbered[:, b, :].rearrange("p (i e) -> p i e", e=2),
                                      -1.0, None, ALU.add)
                step(dve.tensor_reduce(count[:, :], bank[5][:, 32:48], AX_X, ALU.max))
                dve.tensor_copy(fullest[:, l:l + 1], count[:, :]).then_inc(routed, 1)
                dve.wait_ge(routed, l + 1)

            def experts(l, ps, rnd, it):
                s = ps.s
                pairs_before = rnd * PAIRS + it * BODY
                units_before = pairs_before * PAIR_UNITS

                def nth(name, j, k=1, per=1):
                    dve.wait_ge(s[name], pairs_before * per + ((ps.pair0 + j) * per + k))

                def picks(j):
                    if j:
                        nth("pick_t", j - 1)
                    elif ps.rounds > 1:
                        dve.wait_ge(s["renumber"], rnd + 1)
                    pair = it * BODY + j
                    nums = slot[:, bass.ds(pair, 1), :, :].rearrange("p i b e -> p (i b e)")
                    wts = gate[:, bass.ds(pair, 1), :, :].rearrange("p i b e -> p (i b e)")
                    p3 = pick.rearrange("p b (e s) -> p (b e) s", e=2)
                    w3 = pick_w.rearrange("p b (e s) -> p (b e) s", e=2)
                    dve.tensor_tensor(p3, iota.unsqueeze(1).to_broadcast([P, 4, SLOTS]),
                                      nums.unsqueeze(2).to_broadcast([P, 4, SLOTS]), ALU.is_equal)\
                       .then_inc(s["pick"], 1)
                    nth("pick", j, 1, 2)
                    dve.tensor_tensor(w3, p3, wts.unsqueeze(2).to_broadcast([P, 4, SLOTS]), ALU.mult)\
                       .then_inc(s["pick"], 1)

                def add_back(j):
                    for k in range(4):
                        b, n = k // 2, k % 2
                        nth("comb", j, k + 1, 4)
                        a = acc[:, b, n * BANK:(n + 1) * BANK]
                        dve.tensor_tensor(a, a, bank[(7, 4)[k % 2]][:, :], ALU.add).then_inc(s["added"], 1)

                picks(0)
                for j in range(BODY):
                    if j < BODY - 1:
                        picks(j + 1)
                    nth("silu", j)
                    dve.tensor_tensor(hid, silu, bank[3][:, :], ALU.mult).then_inc(s["hid"], 1)
                    if j:
                        add_back(j - 1)
                    nth("hid_t", j)
                    dve.tensor_copy(hidT, bank[4][:, :].rearrange("p (c s) -> p c s", c=FC)).then_inc(s["hidT"], 1)
                add_back(BODY - 1)
                nth("added", BODY - 1, 4, 4)

            dve.wait_ge(x_in, 16 * TB)
            dve.wait_ge(par_in, 32)
            layer_norms(lambda b: h[:, b, :], lambda b: h[:, b, :], ln_par[:, 0, :], ln_par[:, 1, :], D, h_ready)

            for l in range(DEPTH):
                copy_columns(3 * l)
                if l == 0:
                    dve.wait_ge(setup_pe, DEPTH + 1)
                    nt = DEPTH * TAPS + DEPTH
                    dve.tensor_copy(tapsT[:, :, :], bank[3][:, 0:CB * nt].rearrange("p (c k) -> p c k", c=CB))
                    dve.tensor_copy(sgbT[:, :], bank[3][:, 256:256 + DEPTH * GROUPS])
                    for n in range(DEPTH):
                        ins = dve.tensor_copy(sgwT[:, n, :, :], bank[6 + n][:, :].rearrange("p (g t) -> p g t", g=GROUPS))
                    ins.then_inc(setup_copied, 1)
                    dve.wait_ge(setup_copied, 1)
                    dve.wait_ge(pool_const, 4)
                dve.wait_ge(sig_ready, l + 1)
                dve.tensor_tensor(glu[:, :, PAD:PAD + SEQ], bank[4][:, :].rearrange("p (c t) -> p c t", c=CB),
                                  conv_sig, ALU.mult).then_inc(glu_ready, 1)
                dve.wait_ge(glu_ready, l + 1)
                for k in range(TAPS):
                    for cb in range(CB):
                        n = CB * k + cb
                        tap = tapsT[:, cb, l * TAPS + k:l * TAPS + k + 1]
                        src = glu[:, cb, k:k + SEQ]
                        if k == 0:
                            ins = dve.tensor_scalar(conv[:, cb, :], src, tap,
                                                    tapsT[:, cb, DEPTH * TAPS + l:DEPTH * TAPS + l + 1], ALU.mult, ALU.add)
                        else:
                            dve.wait_ge(conv_step, CB * TAPS * l + n - 1)
                            ins = dve.scalar_tensor_tensor(out=conv[:, cb, :], in0=src, scalar=tap,
                                                           in1=conv[:, cb, :], op0=ALU.mult, op1=ALU.add)
                        ins.then_inc(conv_step, 1)
                if l == 0:
                    dve.wait_ge(small_in, 16 * 7)
                    dve.tensor_copy(before_bf[:, :], orders[:, 0:P]).then_inc(casts, 1)
                    dve.tensor_copy(ident_bf[:, :], ident).then_inc(casts, 1)
                    dve.tensor_copy(mask_bf[:, :], orders[:, P:3 * P]).then_inc(casts, 1)
                    dve.wait_ge(casts, 3)
                dve.wait_ge(used, l * LAYER_UNITS + 2)
                rotary_products(l, 0)
                dve.wait_ge(used, l * LAYER_UNITS + 3)
                rotary_products(l, 1)
                dve.wait_ge(convT_pe, l + 1)
                layer_norms(lambda b: bank[4][:, b * CV:(b + 1) * CV], lambda b: mix[:, b, ATT + SG:D],
                            cv_ln[:, l, 0, :], cv_ln[:, l, 1, :], CV, conv_ln_done)
                for b in range(TB):
                    dve.wait_ge(qkT_pe, 4 * l + 2 * b + 2)
                    dve.tensor_copy(qkT[:, 1, :, b * P:(b + 1) * P],
                                    bank[2 + b][:, :].rearrange("p (c t) -> p c t", c=4)).then_inc(qkT_dve, 1)
                dve.wait_ge(gelu_ready, TB * (l + 1))
                layer_norms(lambda b: uv[:, b, SG:2 * SG], lambda b: uv[:, b, SG:2 * SG],
                            sg_ln[:, l, 0, :], sg_ln[:, l, 1, :], SG, sgv_ready)
                for qb in range(TB):
                    for i in range((2, 4)[qb]):
                        dve.wait_ge(scores_pe, 6 * l + 2 * qb + i + 1)
                        if qb == 0:
                            src = bank[6 + i][:, :].rearrange("p (h k) -> p h k", h=4)
                            dst = row_max[:, 0, i::2]
                        else:
                            src = bank[i][:, :].rearrange("p (h k) -> p h k", h=2)
                            dst = row_max[:, 1, 4 * (i // 2) + i % 2:4 * (i // 2) + i % 2 + 3:2]
                        ins = dve.tensor_reduce(dst, src, AX_X, ALU.max)
                    step(ins)
                    dve.tensor_scalar(neg_max[:, qb, :], row_max[:, qb, :], -SCALE, None, ALU.mult).then_inc(max_ready, 1)
                dve.wait_ge(spatial_pe, l + 1)
                for b in range(TB):
                    for g in range(GROUPS):
                        ins = dve.scalar_tensor_tensor(
                            out=mix[:, b, ATT + g * HD:ATT + (g + 1) * HD],
                            in0=bank[4][:, b * SG + g * HD:b * SG + (g + 1) * HD],
                            scalar=sgbT[:, l * GROUPS + g:l * GROUPS + g + 1],
                            in1=uv[:, b, g * HD:(g + 1) * HD], op0=ALU.add, op1=ALU.mult)
                ins.then_inc(sg_out, 1)
                for g in range(6):
                    dve.wait_ge(probT_pe, 6 * l + g + 1)
                    dve.tensor_copy(probT[:, g, :], bank[(g + 6) if g < 2 else g - 2][:, :]).then_inc(probT_ready, 1)
                step(dve.reciprocal(row_inv[:, :, :], row_sum[:, :, :]))
                dve.wait_ge(pv_pe, TB * (l + 1))
                for qb in range(TB):
                    dve.tensor_tensor(mix[:, qb, 0:ATT].rearrange("p (h d) -> p h d", h=HEADS),
                                      bank[4 + qb][:, :].rearrange("p (h d) -> p h d", h=HEADS),
                                      row_inv[:, qb, :].unsqueeze(2).to_broadcast([P, HEADS, HD]), ALU.mult)\
                       .then_inc(att_out, 1)
                copy_columns(3 * l + 1)
                dve.wait_ge(par_in, 32 * (2 * l + 2))
                for b in range(TB):
                    if b == 0:
                        dve.wait_ge(proj_pe, l + 1)
                    else:
                        dve.wait_ge(used, l * LAYER_UNITS + 7)
                    for n in range(2):
                        ins = dve.scalar_tensor_tensor(out=h[:, b, n * BANK:(n + 1) * BANK],
                                                       in0=h[:, b, n * BANK:(n + 1) * BANK], scalar=ALPHA,
                                                       in1=bank[4 + 2 * b + n][:, :], op0=ALU.mult, op1=ALU.add)
                    step(ins)
                    layer_norm(h[:, b, :], h[:, b, :], b, ln_par[:, 0, :], ln_par[:, 1, :], D, h_ready)
                copy_columns(3 * l + 2)
                routing(l)
                dve.wait_ge(acc_init, TB * (l + 1))
                main, more = passes[l]
                with dve.Fori(0, ITERS) as it:
                    experts(l, main, 0, it)
                n = dve.value_load(fullest[0:1, l:l + 1], min_val=0, max_val=SEQ)
                with dve.If(n > SLOTS):
                    with dve.Fori(0, ROUNDS - 1) as rnd:
                        dve.tensor_scalar(slot[:, :, :, :], slot[:, :, :, :], -float(SLOTS), None, ALU.add)\
                           .then_inc(more.s["renumber"], 1)
                        with dve.Fori(0, ITERS) as it:
                            experts(l, more, rnd, it)
                dve.wait_ge(par_in, 32 * (2 * l + 3))
                layer_norms(lambda b: acc[:, b, :], lambda b: h[:, b, :], ln_par[:, 0, :], ln_par[:, 1, :], D, h_ready)


_ORDER = ["x", "ln_in_g", "ln_in_b", "w_in", "w_out", "sg_ln_g", "sg_ln_b", "sg_w", "sg_b", "conv_w", "conv_b",
          "conv_ln_g", "conv_ln_b", "ln_mix_g", "ln_mix_b", "w_router", "router_bias", "w_gate", "w_up", "w_down",
          "ln_ffn_g", "ln_ffn_b"]


def kernel(**inputs):
    import concourse.bacc as bacc
    from concourse.bass_utils import run_bass_kernel_spmd

    nc = bacc.Bacc("TRN2", target_bir_lowering=False, num_devices=1)
    arrays, args = {}, []
    for name in _ORDER:
        a = np.ascontiguousarray(inputs[name])
        arrays[f"in_{name}"] = a
        args.append(nc.dram_tensor(f"in_{name}", a.shape, mybir.dt.from_np(a.dtype), kind="ExternalInput").ap())
    arrays["in_table"] = constants()
    args.append(nc.dram_tensor("in_table", (P, T_COLS), F32, kind="ExternalInput").ap())
    args.append(nc.dram_tensor("out_0", (1, SEQ, D), F32, kind="ExternalOutput").ap())
    trunk(nc, *args)
    r = run_bass_kernel_spmd(nc, [arrays], core_ids=[0])
    return r.results[0]["out_0"]
```

```python
import math
from contextlib import ExitStack

import numpy as np

import concourse.bass as bass
from concourse import mybir

ALU = mybir.AluOpType
ACT = mybir.ActivationFunctionType
AX_X = mybir.AxisListType.X
F32 = mybir.dt.float32
BF16 = mybir.dt.bfloat16
I32 = mybir.dt.int32
F32R = mybir.dt.float32r

P = 128
SEQ = 256
TB = SEQ // P
D = 1024
KC = D // P
DEPTH = 2
HD = 64
HEADS = 8
ATT = HEADS * HD
SG = 256
GROUPS = 4
CV = 256
CB = CV // P
TAPS = 31
PAD = TAPS - 1
EXPERTS = 16
EGROUPS = 4
PER_GROUP = EXPERTS // EGROUPS
DE = 512
FC = DE // P
PAIRS = EXPERTS // 2
SLOTS = 64
ROUNDS = SEQ // SLOTS
EPS = 1e-5
NEG = -1e30
ALPHA = (2.0 * DEPTH) ** 0.25
SCALE = HD ** -0.5
BANK = 512

UNIT = 4096
RING = 8
SLABS = 5 + 2
PAIR_UNITS = 6
LAYER_UNITS = SLABS + PAIR_UNITS * PAIRS
SLAB_COLS = [2048, 0, 512, 1536, 1024]
BODY = 4
TURNS = BODY * PAIR_UNITS // RING
ITERS = PAIRS // BODY
assert BODY * PAIR_UNITS % RING == 0

KEEP_START, KEEP_NORM, KEEP_MIX, KEEP_ROUTER, KEEP_SLOTS = 18, 17, 9, 12, 6

TR_ACT, TR_DVE = TB + 3, TB + 1

T_COS, T_SIN, T_IOTA, T_TIE, T_ID, T_BEFORE, T_MASK = 0, 64, 128, 192, 208, 336, 464
T_COLS = T_MASK + 256
OUT_CHUNKS = [4, 5, 6, 7, 0, 1, 2, 3]
SPLITS = 4
LN_TILES = 4 * TB
COL_NORMS = 2 * DEPTH


def constants():
    t = np.zeros((P, T_COLS), np.float32)
    half = HD // 2
    inv = (10000.0 ** (-np.arange(half, dtype=np.float64) / half)).astype(np.float32)
    ang = np.arange(SEQ, dtype=np.float32)[:, None] * inv[None, :]
    for b in range(TB):
        t[:, T_COS + b * half:T_COS + (b + 1) * half] = np.cos(ang[b * P:(b + 1) * P].astype(np.float64))
        t[:, T_SIN + b * half:T_SIN + (b + 1) * half] = np.sin(ang[b * P:(b + 1) * P].astype(np.float64))
    t[:, T_IOTA:T_IOTA + SLOTS] = 1 + np.arange(SLOTS)
    t[:, T_TIE:T_TIE + 16] = (np.arange(4)[None, :] < np.arange(4)[:, None]).reshape(-1)
    r = np.arange(P)
    t[:, T_ID:T_ID + P] = r[:, None] == r[None, :]
    t[:, T_BEFORE:T_BEFORE + P] = r[:, None] < r[None, :]
    t[:, T_MASK + P:T_MASK + 2 * P] = np.where(r[None, :] > r[:, None], np.float32(NEG), np.float32(0))
    return t


def trunk(nc, x, ln_in_g, ln_in_b, w_in, w_out, sg_ln_g, sg_ln_b, sg_w, sg_b, conv_w, conv_b,
          conv_ln_g, conv_ln_b, ln_mix_g, ln_mix_b, w_router, router_bias, w_gate, w_up, w_down,
          ln_ffn_g, ln_ffn_b, table, out):
    with ExitStack() as ctx:
        def sb(name, shape, dt=F32):
            return ctx.enter_context(nc.sbuf_tensor(name, [P] + shape, dt))

        def sem(name):
            return ctx.enter_context(nc.semaphore(name))

        bank = [ctx.enter_context(nc.psum_tensor(f"bank{i}", [P, BANK], F32)) for i in range(8)]

        ring = sb("ring", [RING, UNIT])
        h = sb("h", [TB, D])
        xT = sb("xT", [KC, SEQ])
        xT_at = nc.sbuf_base - 4 * KC * SEQ
        mix = sb("mix", [TB, D])
        normal = mix
        acc = mix
        area_a = sb("area_a", [3072])
        area_a_at = nc.sbuf_base - 4 * 3072
        area_b = sb("area_b", [3072])
        area_b_at = nc.sbuf_base - 4 * 3072
        uv = sb("uv", [TB, 2 * SG])
        v_rows = mix[:, :, 0:ATT]
        glu = sb("glu", [CB, PAD + SEQ])
        conv = mix[:, 0, 0:CB * SEQ].rearrange("p (c t) -> p c t", c=CB)
        ln_par = sb("ln_par", [2, D])
        col_par = sb("col_par", [COL_NORMS, 2, KC])
        sg_ln = sb("sg_ln", [DEPTH, 2, SG])
        cv_ln = sb("cv_ln", [DEPTH, 2, CV])
        sgwT = sb("sgwT", [DEPTH, GROUPS, P])
        sgbT = sb("sgbT", [DEPTH * GROUPS])
        tapsT = sb("tapsT", [CB, DEPTH * TAPS + DEPTH])
        w_rt = sb("w_rt", [KC, EXPERTS])
        r_bias = sb("r_bias", [EXPERTS])
        tab = sb("tab", [T_BEFORE])
        before_bf = sb("before_bf", [P], BF16)
        ones_bf = sb("ones_bf", [P], BF16)
        ident_bf = sb("ident_bf", [P], BF16)
        mask_bf = sb("mask_bf", [2 * P], BF16)
        half_neg = sb("half_neg", [1])
        stats = sb("stats", [TB, 2, 6])
        mv = sb("mv", [TB, 2])
        n_ln = TB + DEPTH * LN_TILES
        var_eps = sb("var_eps", [n_ln])
        rstd = sb("rstd", [n_ln])
        row_max = sb("row_max", [TB, HEADS])
        neg_max = sb("neg_max", [TB, HEADS])
        row_sum = sb("row_sum", [TB, HEADS])
        row_inv = sb("row_inv", [TB, HEADS])
        gsum = sb("gsum", [3, TB * EGROUPS])
        mask_row = sb("mask_row", [TB, EXPERTS], BF16)
        wsum = sb("wsum", [2, TB])
        fullest = sb("fullest", [DEPTH], I32)
        slot = sb("slot", [PAIRS, TB, 2])
        gate = sb("gate", [PAIRS, TB, 2])

        qk_rows = area_a[:, 0:2048].rearrange("p (b n) -> p b n", b=TB)
        prob0 = area_a[:, 0:1024].rearrange("p (h k) -> p h k", h=HEADS)
        prob1 = area_a[:, 1024:3072].rearrange("p (h k) -> p h k", h=HEADS)
        conv_sig = area_a[:, 2048:2560].rearrange("p (c t) -> p c t", c=CB)
        by_cos = [area_b[:, i * 1024:i * 1024 + 512] for i in range(2)]
        by_sin = [area_b[:, i * 1024 + 512:i * 1024 + 1024] for i in range(2)]
        qkT = area_b[:, 0:2048].rearrange("p (i c t) -> p i c t", i=2, c=HEADS // 2)
        probT = area_b[:, :].rearrange("p (g n) -> p g n", g=6)
        xe = area_a[:, 0:1024].rearrange("p (c s) -> p c s", c=KC)
        silu = area_a[:, 1024:1536]
        hid = area_a[:, 1536:2048]
        hidT = area_a[:, 2048:2560].rearrange("p (c s) -> p c s", c=FC)
        y = area_b[:, 0:1024]
        back = [area_b[:, 1024 + 256 * i:1280 + 256 * i].rearrange("p (b t) -> p b t", b=TB) for i in range(2)]
        pick = area_b[:, 1536:1792].rearrange("p (b s) -> p b s", b=TB)
        pick_w = area_b[:, 1792:2048].rearrange("p (b s) -> p b s", b=TB)
        sgw_rows = area_a[:, 0:1024].rearrange("p (n s) -> p n s", n=DEPTH * GROUPS)
        taps_rows = area_a[0:DEPTH * TAPS + DEPTH, 1024:1280]
        sgb_rows = area_a[0:DEPTH * GROUPS, 1280:1408]
        orders = area_b[:, 0:3 * P]
        cmp = area_b[:, 2048:2048 + 2 * TB * EXPERTS * PER_GROUP].rearrange("p (i n) -> p i n", i=2)
        rt_e, score, biased, rank, sel = (
            area_b[:, 2304 + 32 * i:2336 + 32 * i].rearrange("p (b e) -> p b e", b=TB) for i in range(5))

        x_hi = nc.alloc_sbuf_tensor_at("x_hi", [P, KC, SEQ], F32R, offset=xT_at)
        x_lo = nc.alloc_sbuf_tensor_at("x_lo", [P, KC, SEQ], F32R, offset=area_b_at)
        w_split = [nc.alloc_sbuf_tensor_at(f"w_split{i}", [P, 2, BANK], F32R,
                                           offset=area_a_at + i * 4096 if i < 3 else area_b_at + 8192)
                   for i in range(SPLITS)]

        ident = tab[:, T_ID:T_ID + P]
        iota = tab[:, T_IOTA:T_IOTA + SLOTS]
        tie = tab[:, T_TIE:T_TIE + 16].rearrange("p (i j) -> p i j", i=4)

        x_in = [sem(f"x_in{b}") for b in range(TB)]
        table_in = sem("table_in")
        setup_in = sem("setup_in")
        small_in = sem("small_in")
        par_in = sem("par_in")
        col_par_in = sem("col_par_in")
        out_done = sem("out_done")
        landed = [sem(f"landed{i}") for i in range(RING)]
        first_half_in = sem("first_half_in")
        used = sem("used")
        casts = sem("casts")
        pool_const = sem("pool_const")
        sgw_masked = sem("sgw_masked")
        setup_pe = sem("setup_pe")
        setup_copied = sem("setup_copied")
        norm_ready = sem("norm_ready")
        h_ready = sem("h_ready")
        result_ready = sem("result_ready")
        ln_var = sem("ln_var")
        ln_rstd = sem("ln_rstd")
        tr_pe = sem("tr_pe")
        tr_act = sem("tr_act")
        tr_dve = sem("tr_dve")
        sig_ready = sem("sig_ready")
        gain_step = sem("gain_step")
        gelu_ready = sem("gelu_ready")
        sgv_ready = sem("sgv_ready")
        conv_step = sem("conv_step")
        glu_ready = sem("glu_ready")
        convT_pe = sem("convT_pe")
        spatial_pe = sem("spatial_pe")
        conv_ln_done = sem("conv_ln_done")
        conv_out = sem("conv_out")
        sg_out = sem("sg_out")
        rot_products = sem("rot_products")
        rot_done = sem("rot_done")
        v0_pe = sem("v0_pe")
        v_ready = sem("v_ready")
        qkT_pe = sem("qkT_pe")
        qkT_act = sem("qkT_act")
        qkT_dve = sem("qkT_dve")
        scores_pe = sem("scores_pe")
        max_ready = sem("max_ready")
        exp_done = sem("exp_done")
        probT_pe = sem("probT_pe")
        prob_ready = sem("prob_ready")
        probT_act = sem("probT_act")
        probT_dve = sem("probT_dve")
        proj_pe = sem("proj_pe")
        x_hi_ready = sem("x_hi_ready")
        x_lo_ready = sem("x_lo_ready")
        w_hi_ready = sem("w_hi_ready")
        w_lo_ready = sem("w_lo_ready")
        chunk_used = sem("chunk_used")
        router_pe = sem("router_pe")
        router_exp = sem("router_exp")
        mask_ready = sem("mask_ready")
        before_pe = sem("before_pe")
        routed = sem("routed")
        acc_init = sem("acc_init")
        dve_step = sem("dve_step")

        class Pass:

            def __init__(self, name, used_sem, landed_sems, unit0, used0, pair0, rounds):
                self.unit0 = unit0
                self.load0 = unit0 if rounds == 1 and name == "main" else 0
                self.used0 = used0
                self.pair0 = pair0
                self.rounds = rounds
                self.used = used_sem
                self.landed = landed_sems

        def moe_sems(name):
            return {k: sem(f"{name}_{k}") for k in (
                "pick", "gathered", "pick_t", "xe", "back", "silu", "hid", "hid_t", "hidT", "down_half", "y", "comb", "added", "renumber")}

        main_sems = moe_sems("moe")
        passes = []
        for l in range(DEPTH):
            m = Pass("main", used, landed, l * LAYER_UNITS + SLABS, l * LAYER_UNITS + SLABS, l * PAIRS, 1)
            m.s = main_sems
            more_used = sem(f"more{l}_used")
            more_landed = [sem(f"more{l}_landed{i}") for i in range(RING)]
            o = Pass("more", more_used, more_landed, l * LAYER_UNITS + SLABS, RING, 0, ROUNDS - 1)
            o.s = moe_sems(f"more{l}")
            passes.append((m, o))

        def unit_at(n):
            return ring[:, n % RING, :]

        def wait_unit(pe, n):
            pe.wait_ge(landed[n % RING], 16 * (n // RING + 1))

        def bcast_row(ap1d, n):
            return ap1d.rearrange("(a n) -> a n", a=1).to_broadcast([P, n])

        block = ctx.enter_context(nc.Block())

        @block.sync
        def _(sp):
            for b in range(TB):
                sp.dma_start(h[:, b, :], x[0, b * P:(b + 1) * P, :]).then_inc(x_in[b], 16)
            sp.dma_start(tab[:, :], table[:, 0:T_BEFORE]).then_inc(table_in, 16)
            for i, (src_in, src_mix, src_ffn) in enumerate(((ln_in_g, ln_mix_g, ln_ffn_g), (ln_in_b, ln_mix_b, ln_ffn_b))):
                sp.dma_start(col_par[:, 0, i, :], src_in.rearrange("(p c) -> p c", c=KC)).then_inc(col_par_in, 16)
                sp.dma_start(col_par[:, 1::2, i, :], src_mix.rearrange("l (p c) -> p l c", c=KC)).then_inc(col_par_in, 16)
                sp.dma_start(col_par[:, 2::2, i, :], src_ffn[0:DEPTH - 1].rearrange("l (p c) -> p l c", c=KC))\
                  .then_inc(col_par_in, 16)

            def load_setup():
                sp.dma_start(ln_par[:, 0, :], bcast_row(ln_in_g, D)).then_inc(par_in, 16)
                sp.dma_start(ln_par[:, 1, :], bcast_row(ln_in_b, D)).then_inc(par_in, 16)
                sp.dma_start(taps_rows[0:DEPTH * TAPS, :], conv_w.rearrange("l k c -> (l k) c")).then_inc(setup_in, 16)
                sp.dma_start(taps_rows[DEPTH * TAPS:, :], conv_b).then_inc(setup_in, 16)
                sp.dma_start(sgb_rows, sg_b.rearrange("l g t -> (l g) t")).then_inc(setup_in, 16)
                sp.dma_start(sgw_rows, sg_w.rearrange("l g t s -> t (l g) s")).then_inc(setup_in, 16)

            def load_small():
                sp.dma_start(orders, table[:, T_BEFORE:T_COLS]).then_inc(small_in, 16)
                sp.dma_start(w_rt[:, :, :], w_router.rearrange("(p c) n -> p c n", c=KC)).then_inc(small_in, 16)
                sp.dma_start(r_bias[:, :], bcast_row(router_bias, EXPERTS)).then_inc(small_in, 16)
                for dst, g, s in ((sg_ln, sg_ln_g, sg_ln_b), (cv_ln, conv_ln_g, conv_ln_b)):
                    for i, src in enumerate((g, s)):
                        sp.dma_start(dst[:, :, i, :],
                                     src.rearrange("(a l) n -> a l n", a=1).to_broadcast([P, DEPTH, SG]))\
                          .then_inc(small_in, 16)

            def load_slab(l, i, n):
                if n >= RING:
                    sp.wait_ge(used, n - RING + 1)
                dst = unit_at(n).rearrange("p (c n) -> p c n", c=KC)
                if i < 5:
                    src = w_in[l].rearrange("(p c) n -> p c n", c=KC)[:, :, SLAB_COLS[i]:SLAB_COLS[i] + BANK]
                else:
                    src = w_out[l].rearrange("(c p) n -> p c n", p=P)[:, :, (i - 5) * BANK:(i - 4) * BANK]
                if n == 0:
                    sp.dma_start(dst[:, :, CV:], src[:, :, CV:]).then_inc(first_half_in, 16)
                    sp.dma_start(dst[:, :, 0:CV], src[:, :, 0:CV]).then_inc(landed[0], 16)
                else:
                    sp.dma_start(dst, src).then_inc(landed[n % RING], 16)

            def load_pairs(l, ps, rnd, it):
                for j in range(BODY):
                    first = it * (2 * BODY) + 2 * j
                    for u in range(PAIR_UNITS):
                        k = PAIR_UNITS * j + u
                        turn = rnd * (ITERS * BODY * PAIR_UNITS) + it * (BODY * PAIR_UNITS)
                        sp.wait_ge(ps.used, turn + (ps.used0 + k - RING + 1))
                        half = u // 2 if u < 4 else u - 4
                        if u < 4:
                            w = (w_gate, w_up)[u % 2][l].rearrange("e (p c) n -> p e (c n)", c=KC)
                        else:
                            w = w_down[l].rearrange("e (p c) n -> p e (c n)", c=FC)
                        src = w[:, bass.ds(first, 2), half * 2048:(half + 1) * 2048]
                        at = (ps.unit0 + k) % RING
                        sp.dma_start(ring[:, at, :].rearrange("p (e n) -> p e n", e=2), src)\
                          .then_inc(ps.landed[at], 16)

            for l in range(DEPTH):
                main, more = passes[l]
                for i in range(SLABS):
                    load_slab(l, i, l * LAYER_UNITS + i)
                    if l == 0 and i == 0:
                        load_setup()
                    if l == 0 and i == 1:
                        load_small()
                with sp.Fori(0, ITERS) as it:
                    load_pairs(l, main, 0, it)
                sp.wait_ge(routed, l + 1)
                n = sp.value_load(fullest[0:1, l:l + 1], min_val=0, max_val=SEQ)
                with sp.If(n > SLOTS):
                    sp.wait_ge(used, (l + 1) * LAYER_UNITS)
                    sp.sem_inc(more.used, RING)
                    with sp.Fori(0, ROUNDS - 1) as rnd:
                        with sp.Fori(0, ITERS) as it:
                            load_pairs(l, more, rnd, it)
                    sp.wait_ge(more.used, RING + (ROUNDS - 1) * PAIRS * PAIR_UNITS)
            for b in range(TB):
                sp.wait_ge(result_ready, b + 1)
                sp.dma_start(out[0, b * P:(b + 1) * P, :], h[:, b, :]).then_inc(out_done, 16)
            sp.wait_ge(out_done, 16 * TB)

        @block.tensor
        def _(pe):
            def setup():
                pe.wait_ge(setup_in, 16 * 4)
                pe.wait_ge(sgw_masked, 1)
                nt = DEPTH * TAPS + DEPTH
                for cb in range(CB):
                    pe.transpose(bank[3][:, cb * nt:(cb + 1) * nt], taps_rows[:, cb * P:(cb + 1) * P],
                                 ident[0:nt, 0:nt])
                pe.transpose(bank[3][:, 256:256 + DEPTH * GROUPS], sgb_rows,
                             ident[0:DEPTH * GROUPS, 0:DEPTH * GROUPS]).then_inc(setup_pe, 1)
                for n in range(DEPTH * GROUPS):
                    mm = pe.transpose(bank[6 + n // 4][:, (n % 4) * P:(n % 4 + 1) * P], sgw_rows[:, n, :], ident)
                    if n % 4 == 3:
                        mm.then_inc(setup_pe, 1)

            def keep_clock(at, n):
                for _ in range(n):
                    pe.matmul(bank[at][:, :], ones_bf[:, :], ones_bf[:, :].unsqueeze(1).to_broadcast([P, 4, P]),
                              start=True, stop=True)

            def turn(src, b):
                for half in range(2):
                    dst = bank[2 * b + half]
                    for c in range(4):
                        mm = pe.transpose(dst[:, c * P:(c + 1) * P], src[:, b, 4 * half + c::KC], ident)
                    mm.then_inc(tr_pe, 1)

            def wait_xT(l, stage, b):
                pe.wait_ge(tr_act, TR_ACT * l + (b + 1 if stage == 0 else TB + 2 + b))
                pe.wait_ge(tr_dve, TR_DVE * l + (b + 1 if stage == 0 else TB + b))

            def block_slab(n, b, dst):
                wait_unit(pe, n)
                w = unit_at(n).rearrange("p (c n) -> p c n", c=KC)
                for c in range(KC):
                    mm = pe.matmul(dst[:, :], xT[:, c, b * P:(b + 1) * P], w[:, c, :],
                                   start=c == 0, stop=c == KC - 1)
                if b == TB - 1:
                    mm.then_inc(used, 1)
                return mm

            def product(l, i, b):
                n, k0 = i // KC, i % KC
                if k0 % 4 == 0:
                    pe.wait_ge(x_lo_ready, 2 * TB * l + TB * (k0 // 4) + b + 1)
                pe.wait_ge(w_lo_ready, 2 * KC * l + i + 1)
                w = w_split[i % SPLITS]
                for k, (x, part) in enumerate(((x_hi, 0), (x_hi, 1), (x_lo, 0))):
                    mm = pe.matmul(bank[4 + 2 * b + n][:, :], x[:, k0, b * P:(b + 1) * P], w[:, part, :],
                                   start=k0 == 0 and k == 0, stop=k0 == KC - 1 and k == 2)
                    if k0 == KC - 1 and b == 0 and k == 0:
                        mm.then_inc(used, 1)
                if b == TB - 1:
                    mm.then_inc(chunk_used, 1)
                return mm

            def rows_slab(n, banks):
                for b in range(TB):
                    block_slab(n, b, bank[banks[b]])

            def experts(l, ps, rnd, it):
                s = ps.s
                pairs_before = rnd * PAIRS + it * BODY

                def nth(name, j, k=1, per=1):
                    pe.wait_ge(s[name], pairs_before * per + ((ps.pair0 + j) * per + k))

                def landed_unit(k):
                    at = (ps.unit0 + k) % RING
                    turns = rnd * (ITERS * TURNS * 16) + it * (TURNS * 16)
                    pe.wait_ge(ps.landed[at], turns + 16 * ((ps.load0 + k) // RING + 1))
                    return ring[:, at, :]

                def gather(j, halves=(0, 1)):
                    if 0 in halves:
                        nth("pick", j, 1, 2)
                    for c in range(4 * halves[0], 4 * halves[-1] + 4):
                        for b in range(TB):
                            mm = pe.matmul(bank[c // 4][:, (c % 4) * P:(c % 4 + 1) * P], h[:, b, c::KC],
                                           pick[:, b, :], start=b == 0, stop=b == TB - 1)
                        if c % 4 == 3:
                            mm.then_inc(s["gathered"], 1)
                    if 1 not in halves:
                        return
                    nth("pick", j, 2, 2)
                    if j >= 2:
                        nth("added", j - 2, 3, 4)
                    elif j == 1:
                        nth("back", 0)
                    for b in range(TB):
                        mm = pe.transpose(bank[7][:, b * P:(b + 1) * P], pick_w[:, b, :], ident)
                    mm.then_inc(s["pick_t"], 1)

                def gate_up(j):
                    for u in range(4):
                        if u % 2 == 0:
                            if j == 0 and u == 2:
                                gather(0, (1,))
                            nth("xe", j, u // 2 + 1, 2)
                        w = landed_unit(PAIR_UNITS * j + u).rearrange("p (e c n) -> p e c n", e=2, c=4)
                        for c in range(4):
                            for e in range(2):
                                k = 4 * (u // 2) + c
                                mm = pe.matmul(bank[2 + u % 2][e * SLOTS:(e + 1) * SLOTS, :],
                                               xe[:, k, e * SLOTS:(e + 1) * SLOTS], w[:, e, c, :],
                                               start=k == 0, stop=k == KC - 1)
                        mm.then_inc(ps.used, 1)

                def turn_hid(j):
                    nth("hid", j)
                    for c in range(FC):
                        mm = pe.transpose(bank[2][:, c * P:(c + 1) * P], hid[:, c::FC], ident)
                    mm.then_inc(s["hid_t"], 1)

                def down(j):
                    nth("hidT", j)
                    for u in range(2):
                        w = landed_unit(PAIR_UNITS * j + 4 + u).rearrange("p (e c n) -> p e c n", e=2, c=2)
                        for n in range(2):
                            for c in range(2):
                                for e in range(2):
                                    k = 2 * u + c
                                    mm = pe.matmul(bank[5 + n][e * SLOTS:(e + 1) * SLOTS, :],
                                                   hidT[:, k, e * SLOTS:(e + 1) * SLOTS],
                                                   w[:, e, c, n * BANK:(n + 1) * BANK],
                                                   start=k == 0, stop=k == FC - 1)
                            if u == 1 and n == 0:
                                mm.then_inc(s["down_half"], 1)
                        mm.then_inc(ps.used, 1)

                def combine(j, parts=range(4)):
                    nth("back", min(j + 1, BODY - 1))
                    for k in parts:
                        n, b = k // 2, k % 2
                        if b == 0:
                            nth("y", j, n + 1, 2)
                        if k == 0 and j == BODY - 1:
                            nth("added", j - 1, 3, 4)
                        if k == 1 and j:
                            nth("added", j - 1, 4, 4)
                        if k >= 2:
                            nth("added", j, k - 1, 4)
                        mm = pe.matmul(bank[(7, 4)[k % 2]][:, :], back[j % 2][:, b, :],
                                       y[:, n * BANK:(n + 1) * BANK], start=True, stop=True)
                        mm.then_inc(s["comb"], 1)

                gather(0, (0,))
                for j in range(BODY):
                    gate_up(j)
                    if j == 0:
                        gather(1, (0,))
                    elif j < BODY - 1:
                        combine(j - 1)
                    else:
                        combine(j - 1, (0, 1))
                    turn_hid(j)
                    if j == 0:
                        gather(1, (1,))
                    elif j < BODY - 1:
                        gather(j + 1)
                    else:
                        combine(j - 1, (2, 3))
                    down(j)
                combine(BODY - 1)
                nth("added", BODY - 1, 4, 4)

            pe.wait_ge(pool_const, 3)
            keep_clock(5, KEEP_START)
            pe.wait_ge(table_in, 16)
            for l in range(DEPTH):
                u0 = l * LAYER_UNITS
                if l:
                    keep_clock(5, KEEP_NORM)
                for b in range(TB):
                    pe.wait_ge(norm_ready, 2 * TB * l + b + 1)
                    turn(normal, b)
                wait_xT(l, 0, TB - 1)
                w = unit_at(u0).rearrange("p (c n) -> p c n", c=KC)
                for k in (2, 3, 0, 1):
                    if l == 0 and k == 2:
                        pe.wait_ge(first_half_in, 16)
                    elif k == (2, 0)[l == 0]:
                        wait_unit(pe, u0)
                    for c in range(KC):
                        mm = pe.matmul(bank[4 + k // 2][:, (k % 2) * SEQ:(k % 2 + 1) * SEQ],
                                       w[:, c, k * P:(k + 1) * P], xT[:, c, :], start=c == 0, stop=c == KC - 1)
                mm.then_inc(used, 1)
                if l == 0:
                    setup()
                rows_slab(u0 + 1, (0, 1))
                if l == 0:
                    pe.wait_ge(setup_copied, 1)
                rows_slab(u0 + 2, (2, 3))
                pe.wait_ge(conv_step, CB * TAPS * (l + 1))
                for b in range(TB):
                    for cb in range(CB):
                        mm = pe.transpose(bank[4][:, b * CV + cb * P:b * CV + (cb + 1) * P],
                                          conv[:, cb, b * P:(b + 1) * P], ident)
                mm.then_inc(convT_pe, 1)
                rows_slab(u0 + 3, (6, 7))
                pe.wait_ge(rot_done, 2 * TB * (l + 1))
                for b in range(TB):
                    for i in range(2):
                        for hp in range(HEADS // 2):
                            mm = pe.transpose(bank[2 * i + b][:, hp * P:(hp + 1) * P],
                                              qk_rows[:, b, i * ATT + hp * P:i * ATT + (hp + 1) * P], ident)
                        mm.then_inc(qkT_pe, 1)
                pe.wait_ge(conv_ln_done, TB * (l + 1))
                block_slab(u0 + 4, 0, bank[4]).then_inc(v0_pe, 1)
                pe.wait_ge(gelu_ready, TB * (l + 1))
                pe.wait_ge(qkT_act, 2 * l + 1)
                pe.wait_ge(qkT_dve, 2 * l + 1)
                for par in range(2):
                    pe.matmul(bank[6 + par][:, :], ident_bf[:, :],
                              mask_bf[:, P:2 * P].unsqueeze(1).to_broadcast([P, 4, P]), start=True, stop=False,
                              skip_group_check=True)
                for hp in range(HEADS // 2):
                    for par in range(2):
                        q = slice(par * HD, (par + 1) * HD)
                        mm = pe.matmul(bank[6 + par][:, hp * P:(hp + 1) * P], qkT[q, 0, hp, 0:P], qkT[q, 1, hp, 0:P],
                                       start=False, stop=True, skip_group_check=True)
                        if hp == HEADS // 2 - 1:
                            mm.then_inc(scores_pe, 1)
                pe.wait_ge(qkT_act, 2 * (l + 1))
                pe.wait_ge(qkT_dve, 2 * (l + 1))
                for i in range(4):
                    pe.matmul(bank[i][:, :], ident_bf[:, :],
                              mask_bf[:, :].unsqueeze(1).to_broadcast([P, 2, 2 * P]), start=True, stop=False,
                              skip_group_check=True)
                for hp in range(HEADS // 2):
                    for par in range(2):
                        q = slice(par * HD, (par + 1) * HD)
                        mm = pe.matmul(bank[2 * (hp // 2) + par][:, (hp % 2) * SEQ:(hp % 2 + 1) * SEQ],
                                       qkT[q, 0, hp, P:2 * P], qkT[q, 1, hp, :],
                                       start=False, stop=True, skip_group_check=True)
                        if hp % 2 == 1:
                            mm.then_inc(scores_pe, 1)
                pe.wait_ge(v_ready, TB * l + 1)
                for b in range(TB):
                    pe.wait_ge(sgv_ready, TB * l + b + 1)
                    for g in range(GROUPS):
                        mm = pe.matmul(bank[4][:, b * SG + g * HD:b * SG + (g + 1) * HD], sgwT[:, l, g, :],
                                       uv[:, b, SG + g * HD:SG + (g + 1) * HD], start=True, stop=True)
                mm.then_inc(spatial_pe, 1)
                block_slab(u0 + 4, 1, bank[5])
                for g in range(6):
                    pe.wait_ge(prob_ready, 3 * l + g // 2 + 1)
                    for i in range(4):
                        src = prob0[:, 4 * g + i, :] if g < 2 else prob1[:, 2 * g - 4 + i // 2, (i % 2) * P:(i % 2 + 1) * P]
                        mm = pe.transpose(bank[(g + 6) % 8][:, i * P:(i + 1) * P], src, ident)
                    mm.then_inc(probT_pe, 1)
                pe.wait_ge(sg_out, l + 1)
                pe.wait_ge(conv_out, l + 1)
                pe.wait_ge(v_ready, TB * (l + 1))
                for b in range(TB):
                    if b == 1:
                        pe.wait_ge(probT_act, 3 * l + 1)
                    for i in range(4):
                        mm = pe.transpose(bank[5 + 2 * b][:, i * P:(i + 1) * P], mix[:, b, ATT + i * P:ATT + (i + 1) * P], ident)
                    mm.then_inc(tr_pe, 1)
                pe.wait_ge(probT_dve, 3 * l + 2)
                for hd in range(HEADS):
                    hp, e = hd // 2, hd % 2
                    mm = pe.matmul(bank[0][e * HD:(e + 1) * HD, hp * P:(hp + 1) * P], v_rows[:, 0, hd * HD:(hd + 1) * HD],
                                   probT[:, hd // 4, (hd % 4) * P:(hd % 4 + 1) * P], start=True, stop=True)
                mm.then_inc(tr_pe, 1)
                pe.wait_ge(probT_act, 3 * l + 2)
                for hp in range(HEADS // 2):
                    pe.wait_ge((probT_dve, probT_act)[hp % 2], 3 * l + 2 + hp // 2)
                    for kb in range(TB):
                        for e in range(2):
                            hd = 2 * hp + e
                            i = 2 * e + kb
                            mm = pe.matmul(bank[1][e * HD:(e + 1) * HD, hp * P:(hp + 1) * P],
                                           v_rows[:, kb, hd * HD:(hd + 1) * HD], probT[:, 2 + hp, i * P:(i + 1) * P],
                                           start=kb == 0, stop=kb == 1)
                mm.then_inc(tr_pe, 1)
                for c in range(2 * KC - SPLITS):
                    for b in range(TB):
                        product(l, c, b)
                for b in range(TB):
                    for c in range(2 * KC - SPLITS, 2 * KC):
                        mm = product(l, c, b)
                    if b == 0:
                        mm.then_inc(proj_pe, 1)
                for b in range(TB):
                    pe.wait_ge(norm_ready, 2 * TB * l + TB + b + 1)
                    turn(normal, b)
                    if b == 0:
                        keep_clock(5, KEEP_MIX)
                if l == 0:
                    pe.wait_ge(small_in, 16 * 7)
                for b in range(TB):
                    wait_xT(l, 2, b)
                    for c in range(KC):
                        mm = pe.matmul(bank[4][:, b * EXPERTS:(b + 1) * EXPERTS], xT[:, c, b * P:(b + 1) * P],
                                       w_rt[:, c, :], start=c == 0, stop=c == KC - 1)
                mm.then_inc(router_pe, 1)
                keep_clock(7, KEEP_ROUTER)
                pe.wait_ge(mask_ready, l + 1)
                pe.wait_ge(casts, 3)
                pe.matmul(bank[5][:, 0:16], before_bf[:, :], mask_row[:, 0, :], start=True, stop=True)
                pe.matmul(bank[5][:, 16:32], ones_bf[:, :], mask_row[:, 0, :], start=True, stop=False)
                pe.matmul(bank[5][:, 16:32], before_bf[:, :], mask_row[:, 1, :], start=False, stop=True)
                pe.matmul(bank[5][:, 32:48], ones_bf[:, :], mask_row[:, 0, :], start=True, stop=False)
                pe.matmul(bank[5][:, 32:48], ones_bf[:, :], mask_row[:, 1, :], start=False, stop=True)\
                  .then_inc(before_pe, 1)
                keep_clock(7, KEEP_SLOTS)
                main, more = passes[l]
                pe.wait_ge(h_ready, 2 * TB * (l + 1))
                with pe.Fori(0, ITERS) as it:
                    experts(l, main, 0, it)
                pe.wait_ge(routed, l + 1)
                n = pe.value_load(fullest[0:1, l:l + 1], min_val=0, max_val=SEQ)
                with pe.If(n > SLOTS):
                    with pe.Fori(0, ROUNDS - 1) as rnd:
                        with pe.Fori(0, ITERS) as it:
                            experts(l, more, rnd, it)

        @block.scalar
        def _(act):
            def next_params(gain, shift, free_after):
                act.wait_ge(h_ready, free_after)
                act.dma_start(ln_par[:, 0, :], bcast_row(gain, D)).then_inc(par_in, 16)
                act.dma_start(ln_par[:, 1, :], bcast_row(shift, D)).then_inc(par_in, 16)

            def scaled_columns(stage, norm, parts):
                for b, half in parts:
                    act.wait_ge(tr_pe, 4 * stage + 2 * b + half + 1)
                    for i in range(4):
                        c = 4 * half + i
                        ins = act.activation(xT[:, c, b * P:(b + 1) * P], bank[2 * b + half][:, i * P:(i + 1) * P],
                                             ACT.Identity, scale=col_par[:, norm, 0, c:c + 1],
                                             bias=col_par[:, norm, 1, c:c + 1])
                    ins.then_inc(tr_act, 1)

            def w_high(l, i):
                n = l * LAYER_UNITS + 5 + i // KC
                if i % KC == 0:
                    act.wait_ge(landed[n % RING], 16 * (n // RING + 1))
                if i >= SPLITS:
                    act.wait_ge(chunk_used, 2 * KC * l + i - SPLITS + 1)
                c = OUT_CHUNKS[i % KC]
                act.activation(w_split[i % SPLITS][:, 0, :], unit_at(n)[:, c * BANK:(c + 1) * BANK], ACT.Copy)\
                   .then_inc(w_hi_ready, 1)

            def x_high(l):
                for half in range(2):
                    for b in range(TB):
                        act.wait_ge(tr_pe, 4 * (3 * l + 1) + TB * half + b + 1)
                        act.activation(x_hi[:, 4 * half:4 * half + 4, b * P:(b + 1) * P],
                                       bank[(5 + 2 * b, b)[half]][:, :].rearrange("p (c t) -> p c t", c=4), ACT.Copy)\
                           .then_inc(x_hi_ready, 1)

            def experts(l, ps, rnd, it):
                s = ps.s
                pairs_before = rnd * PAIRS + it * BODY
                units_before = pairs_before * PAIR_UNITS

                def nth(name, j, k=1, per=1):
                    act.wait_ge(s[name], pairs_before * per + ((ps.pair0 + j) * per + k))

                def tokens(j):
                    for half in range(2):
                        nth("gathered", j, half + 1, 2)
                        act.activation(xe[:, 4 * half:4 * half + 4, :],
                                       bank[half][:, :].rearrange("p (c s) -> p c s", c=4), ACT.Copy)\
                           .then_inc(s["xe"], 1)
                    nth("pick_t", j)
                    act.activation(back[j % 2], bank[7][:, 0:SEQ].rearrange("p (b t) -> p b t", b=TB), ACT.Copy)\
                       .then_inc(s["back"], 1)

                tokens(0)
                for j in range(BODY):
                    act.wait_ge(ps.used, units_before + (ps.used0 + PAIR_UNITS * j + 4))
                    act.activation(silu, bank[2][:, :], ACT.Silu).then_inc(s["silu"], 1)
                    if j < BODY - 1:
                        tokens(j + 1)
                    for n in range(2):
                        if n == 0:
                            nth("down_half", j)
                        else:
                            act.wait_ge(ps.used, units_before + (ps.used0 + PAIR_UNITS * (j + 1)))
                        act.activation(y[:, n * BANK:(n + 1) * BANK], bank[5 + n][:, :], ACT.Copy)\
                           .then_inc(s["y"], 1)

            act.preload_act_table(ACT.Identity)
            act.wait_ge(col_par_in, 16 * 6)
            for l in range(DEPTH):
                scaled_columns(3 * l, 2 * l, [(0, 0), (1, 0)])
                act.wait_ge(used, l * LAYER_UNITS + 1)
                act.activation(conv_sig, bank[5][:, :].rearrange("p (c t) -> p c t", c=CB), ACT.Sigmoid)\
                   .then_inc(sig_ready, 1)
                next_params(ln_mix_g[l], ln_mix_b[l], 2 * TB * l + TB)
                act.wait_ge(conv_ln_done, TB * (l + 1))
                act.activation(mix[:, :, ATT + SG:D], mix[:, :, ATT + SG:D], ACT.Silu).then_inc(conv_out, 1)
                act.wait_ge(used, l * LAYER_UNITS + 4)
                for b in range(TB):
                    act.activation(uv[:, b, :], bank[6 + b][:, :], ACT.Gelu_apprx_tanh).then_inc(gelu_ready, 1)
                for b in range(TB):
                    act.wait_ge(qkT_pe, 4 * l + 2 * b + 1)
                    act.activation(qkT[:, 0, :, b * P:(b + 1) * P],
                                   bank[b][:, :].rearrange("p (c t) -> p c t", c=4), ACT.Copy).then_inc(qkT_act, 1)
                act.wait_ge(v0_pe, l + 1)
                act.activation(v_rows[:, 0, :], bank[4][:, :], ACT.Copy).then_inc(v_ready, 1)
                for qb in range(TB):
                    act.wait_ge(max_ready, TB * l + qb + 1)
                    for hd in range(HEADS):
                        if qb == 0:
                            src, dst = bank[6 + hd % 2][:, (hd // 2) * P:(hd // 2 + 1) * P], prob0[:, hd, :]
                        else:
                            src = bank[2 * (hd // 4) + hd % 2][:, (hd // 2 % 2) * SEQ:(hd // 2 % 2 + 1) * SEQ]
                            dst = prob1[:, hd, :]
                        act.activation(dst, src, ACT.Exp, bias=neg_max[:, qb, hd:hd + 1], scale=SCALE,
                                       accum_out=row_sum[:, qb, hd:hd + 1]).then_inc(exp_done, 1)
                act.wait_ge(used, l * LAYER_UNITS + 5)
                act.activation(v_rows[:, 1, :], bank[5][:, :], ACT.Copy).then_inc(v_ready, 1)
                for g in (1, 3, 5):
                    act.wait_ge(probT_pe, 6 * l + g + 1)
                    act.activation(probT[:, g, :], bank[(g + 6) % 8][:, :], ACT.Copy).then_inc(probT_act, 1)
                act.wait_ge(probT_pe, 6 * (l + 1))
                for i in range(SPLITS - 1):
                    w_high(l, i)
                x_high(l)
                act.wait_ge(tr_pe, 4 * (3 * l + 2))
                for i in range(SPLITS - 1, 2 * KC):
                    w_high(l, i)
                scaled_columns(3 * l + 2, 2 * l + 1, [(0, 0), (0, 1), (1, 0)])
                act.wait_ge(router_pe, l + 1)
                act.activation(rt_e[:, :, :], bank[4][:, 0:TB * EXPERTS].rearrange("p (b e) -> p b e", b=TB),
                               ACT.Exp, scale=-1.0).then_inc(router_exp, 1)
                next_params(ln_ffn_g[l], ln_ffn_b[l], 2 * TB * l + 2 * TB)
                main, more = passes[l]
                with act.Fori(0, ITERS) as it:
                    experts(l, main, 0, it)
                act.wait_ge(routed, l + 1)
                n = act.value_load(fullest[0:1, l:l + 1], min_val=0, max_val=SEQ)
                with act.If(n > SLOTS):
                    with act.Fori(0, ROUNDS - 1) as rnd:
                        with act.Fori(0, ITERS) as it:
                            experts(l, more, rnd, it)

        @block.gpsimd
        def _(pool):
            norms = [0]

            def inverse_deviations(n):
                for _ in range(n):
                    i = norms[0]
                    norms[0] += 1
                    pool.wait_ge(ln_var, i + 1)
                    pool.tensor_tensor(rstd[:, i:i + 1], var_eps[:, i:i + 1], half_neg[:, :], ALU.pow)\
                        .then_inc(ln_rstd, 1)

            pool.memset(half_neg[:, :], -0.5).then_inc(pool_const, 1)
            pool.memset(ones_bf[:, :], 1.0).then_inc(pool_const, 1)
            pool.memset(glu[:, :, 0:PAD], 0.0).then_inc(pool_const, 1)
            pool.wait_ge(pool_const, 3)
            inverse_deviations(TB)
            pool.wait_ge(setup_in, 16 * 4)
            pool.affine_select(out=sgw_rows, in_=sgw_rows, compare_op=ALU.is_ge, fill=0.0, base=0,
                               pattern=[[0, DEPTH * GROUPS], [-1, P]], channel_multiplier=1).then_inc(sgw_masked, 1)

            products = [0]

            def gain_and_shift(b, first):
                pool.wait_ge(norm_ready, first + b + 1)
                pool.wait_ge(par_in, 32 * (first // TB + 1))
                pool.tensor_tensor(h[:, b, :], normal[:, b, :], ln_par[:, 0, :], ALU.mult).then_inc(gain_step, 1)
                products[0] += 1
                pool.wait_ge(gain_step, products[0])
                pool.tensor_tensor(h[:, b, :], h[:, b, :], ln_par[:, 1, :], ALU.add).then_inc(h_ready, 1)

            def rotate(l, i):
                for b in range(TB):
                    pool.wait_ge(rot_products, 2 * TB * l + 2 * i + b + 1)
                    a = by_cos[b].rearrange("p (h x d) -> p h x d", h=HEADS, x=2)
                    s = by_sin[b].rearrange("p (h x d) -> p h x d", h=HEADS, x=2)
                    o = qk_rows[:, b, i * ATT:(i + 1) * ATT].rearrange("p (h x d) -> p h x d", h=HEADS, x=2)
                    pool.tensor_tensor(o[:, :, 0, :], a[:, :, 0, :], s[:, :, 1, :], ALU.subtract)
                    pool.tensor_tensor(o[:, :, 1, :], a[:, :, 1, :], s[:, :, 0, :], ALU.add).then_inc(rot_done, 1)

            for l in range(DEPTH):
                for b in range(TB):
                    gain_and_shift(b, 2 * TB * l)
                rotate(l, 0)
                rotate(l, 1)
                inverse_deviations(TB)
                inverse_deviations(TB)
                inverse_deviations(TB)
                for b in range(TB):
                    gain_and_shift(b, 2 * TB * l + TB)
                for b in range(TB):
                    pool.wait_ge(tr_pe, 4 * (3 * l + 2) + 2 * b + 2)
                    pool.wait_ge(h_ready, 2 * TB * l + TB + b + 1)
                    pool.tensor_scalar(acc[:, b, :], h[:, b, :], ALPHA, 1.0, ALU.mult, ALU.mult).then_inc(acc_init, 1)
                inverse_deviations(TB)

        @block.vector
        def _(dve):
            steps = [0]

            def step(ins):
                steps[0] += 1
                ins.then_inc(dve_step, 1)
                dve.wait_ge(dve_step, steps[0])

            norms = [0]

            def norm_stats(src, b, width):
                parts = max(1, width // BANK)
                w = width // parts
                for k in range(parts):
                    ins = dve.bn_stats(stats[:, b, k, :], src[:, k * w:(k + 1) * w])
                step(ins)
                return norm_variance(b, parts)

            def norm_variance(b, parts):
                i = norms[0]
                norms[0] += 1
                step(dve.bn_aggr(mv[:, b, :], stats[:, b, 0:parts, :]))
                dve.tensor_scalar(var_eps[:, i:i + 1], mv[:, b, 1:2], EPS, None, ALU.add).then_inc(ln_var, 1)
                return i

            def norm_apply(i, src, dst, b, gain, shift, signal):
                step(dve.scalar_tensor_tensor(out=dst, in0=src, scalar=mv[:, b, 0:1], in1=gain,
                                              op0=ALU.subtract, op1=ALU.mult))
                dve.wait_ge(ln_rstd, i + 1)
                dve.scalar_tensor_tensor(out=dst, in0=dst, scalar=rstd[:, i:i + 1], in1=shift,
                                         op0=ALU.mult, op1=ALU.add).then_inc(signal, 1)

            def norm_center(i, src, b):
                dve.wait_ge(ln_rstd, i + 1)
                dve.tensor_scalar(normal[:, b, :], src, mv[:, b, 0:1], rstd[:, i:i + 1], ALU.subtract, ALU.mult)\
                   .then_inc(norm_ready, 1)

            def layer_norms(src, dst, gain, shift, width, signal):
                i = [norm_stats(src(b), b, width) for b in range(TB)]
                for b in range(TB):
                    norm_apply(i[b], src(b), dst(b), b, gain, shift, signal)

            def scaled_columns(stage, norm, blocks=range(TB)):
                for b in blocks:
                    dve.wait_ge(tr_pe, 4 * stage + 2 * b + 2)
                    for c in range(4):
                        ins = dve.tensor_scalar(xT[:, 4 + c, b * P:(b + 1) * P], bank[2 * b + 1][:, c * P:(c + 1) * P],
                                                col_par[:, norm, 0, 4 + c:5 + c], col_par[:, norm, 1, 4 + c:5 + c],
                                                ALU.mult, ALU.add)
                    ins.then_inc(tr_dve, 1)

            def w_low(l, i):
                dve.wait_ge(w_hi_ready, 2 * KC * l + i + 1)
                w, c = w_split[i % SPLITS], OUT_CHUNKS[i % KC]
                dve.tensor_tensor(w[:, 1, :], unit_at(l * LAYER_UNITS + 5 + i // KC)[:, c * BANK:(c + 1) * BANK],
                                  w[:, 0, :].bitcast(F32), ALU.subtract).then_inc(w_lo_ready, 1)

            def x_low(l):
                for half in range(2):
                    dve.wait_ge(tr_pe, 4 * (3 * l + 1) + 3 + half)
                    for b in range(TB):
                        dve.wait_ge(x_hi_ready, 2 * TB * l + TB * half + b + 1)
                        dve.tensor_tensor(x_lo[:, 4 * half:4 * half + 4, b * P:(b + 1) * P],
                                          bank[(5 + 2 * b, b)[half]][:, :].rearrange("p (c t) -> p c t", c=4),
                                          x_hi[:, 4 * half:4 * half + 4, b * P:(b + 1) * P].bitcast(F32), ALU.subtract)\
                           .then_inc(x_lo_ready, 1)

            def over_sums(l, qb, h0, h1):
                dve.wait_ge(exp_done, 2 * HEADS * l + HEADS * qb + h1)
                step(dve.reciprocal(row_inv[:, qb, h0:h1], row_sum[:, qb, h0:h1]))
                e = (prob0, prob1)[qb][:, h0:h1, :]
                dve.tensor_tensor(e, e, row_inv[:, qb, h0:h1].unsqueeze(2).to_broadcast([P, h1 - h0, (qb + 1) * P]),
                                  ALU.mult).then_inc(prob_ready, 1)

            def residual(l, b, n):
                half = h[:, b, n * BANK:(n + 1) * BANK]
                step(dve.scalar_tensor_tensor(out=half, in0=half, scalar=ALPHA, in1=bank[4 + 2 * b + n][:, :],
                                              op0=ALU.mult, op1=ALU.add))
                return dve.bn_stats(stats[:, b, n, :], half)

            def rotary_products(l, i):
                for b in range(TB):
                    src = bank[2 * i + b][:, :].rearrange("p (h d) -> p h d", d=HD // 2)
                    if i == 1:
                        dve.wait_ge(rot_done, 2 * TB * l + b + 1)
                    for t0, dst in ((T_COS, by_cos[b]), (T_SIN, by_sin[b])):
                        angle = tab[:, t0 + b * 32:t0 + (b + 1) * 32].unsqueeze(1).to_broadcast([P, 16, 32])
                        ins = dve.tensor_tensor(dst.rearrange("p (h d) -> p h d", d=HD // 2), src, angle, ALU.mult)
                    ins.then_inc(rot_products, 1)

            def routing(l):
                sc = score[:, :, :].rearrange("p b e -> p (b e)")
                bi = biased[:, :, :].rearrange("p b e -> p (b e)")
                se = sel[:, :, :].rearrange("p b e -> p (b e)")
                ra = rank[:, :, :].rearrange("p b e -> p (b e)")
                ex = rt_e[:, :, :].rearrange("p b e -> p (b e)")
                dve.wait_ge(router_exp, l + 1)
                step(dve.tensor_scalar(ex, ex, 1.0, None, ALU.add))
                step(dve.reciprocal(sc, ex))
                step(dve.tensor_tensor(biased[:, :, :], score[:, :, :],
                                       r_bias[:, :].unsqueeze(1).to_broadcast([P, TB, EXPERTS]), ALU.add))

                def ranks(v, n, m, dst):
                    them = v.rearrange("p (g j) -> p g j", j=m).unsqueeze(2).to_broadcast([P, n, m, m])
                    one = v.rearrange("p (g j) -> p g j", j=m).unsqueeze(3).to_broadcast([P, n, m, m])
                    c0 = cmp[:, 0, 0:n * m * m].rearrange("p (g i j) -> p g i j", i=m, j=m)
                    c1 = cmp[:, 1, 0:n * m * m].rearrange("p (g i j) -> p g i j", i=m, j=m)
                    dve.tensor_tensor(c0, them, one, ALU.is_gt)
                    step(dve.tensor_tensor(c1, them, one, ALU.is_equal))
                    step(dve.tensor_tensor(c1, c1, tie.unsqueeze(1).to_broadcast([P, n, m, m]), ALU.mult))
                    step(dve.tensor_tensor(c0, c0, c1, ALU.add))
                    step(dve.tensor_reduce(dst, c0, AX_X, ALU.add))

                ranks(bi, TB * EGROUPS, PER_GROUP, ra.rearrange("p (g j) -> p g j", j=PER_GROUP))
                dve.tensor_scalar(se, ra, 2.0, None, ALU.is_lt)
                step(dve.scalar_tensor_tensor(out=ex, in0=ra, scalar=2.0, in1=bi, op0=ALU.is_lt, op1=ALU.mult))
                step(dve.tensor_reduce(gsum[:, 0, :], ex.rearrange("p (g j) -> p g j", j=PER_GROUP), AX_X, ALU.add))
                ranks(gsum[:, 0, :], TB, EGROUPS, gsum[:, 1, :].rearrange("p (g j) -> p g j", j=EGROUPS))
                chosen = mask_row[:, :, :].rearrange("p b (g j) -> p (b g) j", j=PER_GROUP)
                dve.scalar_tensor_tensor(out=chosen, in0=gsum[:, 1, :].unsqueeze(2).to_broadcast([P, TB * EGROUPS, PER_GROUP]),
                                         scalar=1.0, in1=se.rearrange("p (g j) -> p g j", j=PER_GROUP),
                                         op0=ALU.is_lt, op1=ALU.mult).then_inc(mask_ready, 1)
                dve.wait_ge(mask_ready, l + 1)
                step(dve.tensor_tensor(ra, mask_row[:, :, :].rearrange("p b e -> p (b e)"), sc, ALU.mult))
                step(dve.tensor_reduce(wsum[:, 0, :], rank[:, :, :], AX_X, ALU.add))
                step(dve.reciprocal(wsum[:, 1, :], wsum[:, 0, :]))
                for b in range(TB):
                    dve.tensor_scalar(gate[:, :, b, :], rank[:, b, :].rearrange("p (i e) -> p i e", e=2),
                                      wsum[:, 1, b:b + 1], None, ALU.mult)
                dve.wait_ge(before_pe, l + 1)
                for b in range(TB):
                    dve.scalar_tensor_tensor(out=slot[:, :, b, :],
                                             in0=bank[5][:, b * 16:(b + 1) * 16].rearrange("p (i e) -> p i e", e=2), scalar=1.0,
                                             in1=mask_row[:, b, :].rearrange("p (i e) -> p i e", e=2),
                                             op0=ALU.add, op1=ALU.mult)
                dve.tensor_reduce(fullest[:, l:l + 1], bank[5][:, 32:48], AX_X, ALU.max).then_inc(routed, 1)
                dve.wait_ge(routed, l + 1)

            def experts(l, ps, rnd, it):
                s = ps.s
                pairs_before = rnd * PAIRS + it * BODY

                def nth(name, j, k=1, per=1):
                    dve.wait_ge(s[name], pairs_before * per + ((ps.pair0 + j) * per + k))

                def picks(j):
                    if j:
                        nth("pick_t", j - 1)
                    elif ps.rounds > 1:
                        dve.wait_ge(s["renumber"], rnd + 1)
                    pair = it * BODY + j
                    nums = slot[:, bass.ds(pair, 1), :, :].rearrange("p i b e -> p (i b e)")
                    wts = gate[:, bass.ds(pair, 1), :, :].rearrange("p i b e -> p (i b e)")
                    p3 = pick.rearrange("p b (e s) -> p (b e) s", e=2)
                    w3 = pick_w.rearrange("p b (e s) -> p (b e) s", e=2)
                    dve.tensor_tensor(p3, iota.unsqueeze(1).to_broadcast([P, 4, SLOTS]),
                                      nums.unsqueeze(2).to_broadcast([P, 4, SLOTS]), ALU.is_equal)\
                       .then_inc(s["pick"], 1)
                    nth("pick", j, 1, 2)
                    dve.tensor_tensor(w3, p3, wts.unsqueeze(2).to_broadcast([P, 4, SLOTS]), ALU.mult)\
                       .then_inc(s["pick"], 1)

                def add_back(j, parts=range(4)):
                    for k in parts:
                        n, b = k // 2, k % 2
                        nth("comb", j, k + 1, 4)
                        a = acc[:, b, n * BANK:(n + 1) * BANK]
                        dve.tensor_tensor(a, a, bank[(7, 4)[k % 2]][:, :], ALU.add).then_inc(s["added"], 1)

                picks(0)
                for j in range(BODY):
                    if j < BODY - 1:
                        picks(j + 1)
                    nth("silu", j)
                    dve.tensor_tensor(hid, silu, bank[3][:, :], ALU.mult).then_inc(s["hid"], 1)
                    if j:
                        add_back(j - 1, (0, 1) if j == BODY - 1 else range(4))
                    nth("hid_t", j)
                    dve.tensor_copy(hidT, bank[2][:, :].rearrange("p (c s) -> p c s", c=FC)).then_inc(s["hidT"], 1)
                    if j == BODY - 1:
                        add_back(j - 1, (2, 3))
                add_back(BODY - 1)
                nth("added", BODY - 1, 4, 4)

            x_norm = []
            for b in range(TB):
                dve.wait_ge(x_in[b], 16)
                x_norm.append(norm_stats(h[:, b, :], b, D))
            for b in range(TB):
                norm_center(x_norm[b], h[:, b, :], b)
            dve.wait_ge(col_par_in, 16 * 6)

            for l in range(DEPTH):
                scaled_columns(3 * l, 2 * l)
                if l == 0:
                    dve.wait_ge(setup_pe, DEPTH + 1)
                    nt = DEPTH * TAPS + DEPTH
                    dve.tensor_copy(tapsT[:, :, :], bank[3][:, 0:CB * nt].rearrange("p (c k) -> p c k", c=CB))
                    dve.tensor_copy(sgbT[:, :], bank[3][:, 256:256 + DEPTH * GROUPS])
                    for n in range(DEPTH):
                        ins = dve.tensor_copy(sgwT[:, n, :, :], bank[6 + n][:, :].rearrange("p (g t) -> p g t", g=GROUPS))
                    ins.then_inc(setup_copied, 1)
                    dve.wait_ge(setup_copied, 1)
                    dve.wait_ge(pool_const, 3)
                dve.wait_ge(sig_ready, l + 1)
                dve.tensor_tensor(glu[:, :, PAD:PAD + SEQ], bank[4][:, :].rearrange("p (c t) -> p c t", c=CB),
                                  conv_sig, ALU.mult).then_inc(glu_ready, 1)
                dve.wait_ge(glu_ready, l + 1)
                dve.wait_ge(h_ready, 2 * TB * l + TB)
                for k in range(TAPS):
                    for cb in range(CB):
                        n = CB * k + cb
                        tap = tapsT[:, cb, l * TAPS + k:l * TAPS + k + 1]
                        src = glu[:, cb, k:k + SEQ]
                        if k == 0:
                            ins = dve.tensor_scalar(conv[:, cb, :], src, tap,
                                                    tapsT[:, cb, DEPTH * TAPS + l:DEPTH * TAPS + l + 1], ALU.mult, ALU.add)
                        else:
                            dve.wait_ge(conv_step, CB * TAPS * l + n - 1)
                            ins = dve.scalar_tensor_tensor(out=conv[:, cb, :], in0=src, scalar=tap,
                                                           in1=conv[:, cb, :], op0=ALU.mult, op1=ALU.add)
                        ins.then_inc(conv_step, 1)
                if l == 0:
                    dve.wait_ge(small_in, 16 * 7)
                    dve.tensor_copy(before_bf[:, :], orders[:, 0:P]).then_inc(casts, 1)
                    dve.tensor_copy(ident_bf[:, :], ident).then_inc(casts, 1)
                    dve.tensor_copy(mask_bf[:, :], orders[:, P:3 * P]).then_inc(casts, 1)
                    dve.wait_ge(casts, 3)
                dve.wait_ge(used, l * LAYER_UNITS + 2)
                rotary_products(l, 0)
                dve.wait_ge(used, l * LAYER_UNITS + 3)
                rotary_products(l, 1)
                dve.wait_ge(convT_pe, l + 1)
                layer_norms(lambda b: bank[4][:, b * CV:(b + 1) * CV], lambda b: mix[:, b, ATT + SG:D],
                            cv_ln[:, l, 0, :], cv_ln[:, l, 1, :], CV, conv_ln_done)
                for b in range(TB):
                    dve.wait_ge(qkT_pe, 4 * l + 2 * b + 2)
                    dve.tensor_copy(qkT[:, 1, :, b * P:(b + 1) * P],
                                    bank[2 + b][:, :].rearrange("p (c t) -> p c t", c=4)).then_inc(qkT_dve, 1)
                dve.wait_ge(gelu_ready, TB * (l + 1))
                layer_norms(lambda b: uv[:, b, SG:2 * SG], lambda b: uv[:, b, SG:2 * SG],
                            sg_ln[:, l, 0, :], sg_ln[:, l, 1, :], SG, sgv_ready)
                for qb in range(TB):
                    for i in range((2, 4)[qb]):
                        dve.wait_ge(scores_pe, 6 * l + 2 * qb + i + 1)
                        if qb == 0:
                            src = bank[6 + i][:, :].rearrange("p (h k) -> p h k", h=4)
                            dst = row_max[:, 0, i::2]
                        else:
                            src = bank[i][:, :].rearrange("p (h k) -> p h k", h=2)
                            dst = row_max[:, 1, 4 * (i // 2) + i % 2:4 * (i // 2) + i % 2 + 3:2]
                        ins = dve.tensor_reduce(dst, src, AX_X, ALU.max)
                    step(ins)
                    dve.tensor_scalar(neg_max[:, qb, :], row_max[:, qb, :], -SCALE, None, ALU.mult).then_inc(max_ready, 1)
                over_sums(l, 0, 0, HEADS)
                dve.wait_ge(spatial_pe, l + 1)
                for b in range(TB):
                    for g in range(GROUPS):
                        ins = dve.scalar_tensor_tensor(
                            out=mix[:, b, ATT + g * HD:ATT + (g + 1) * HD],
                            in0=bank[4][:, b * SG + g * HD:b * SG + (g + 1) * HD],
                            scalar=sgbT[:, l * GROUPS + g:l * GROUPS + g + 1],
                            in1=uv[:, b, g * HD:(g + 1) * HD], op0=ALU.add, op1=ALU.mult)
                ins.then_inc(sg_out, 1)
                over_sums(l, 1, 0, HEADS // 2)
                over_sums(l, 1, HEADS // 2, HEADS)
                for g in (0, 2, 4):
                    dve.wait_ge(probT_pe, 6 * l + g + 1)
                    dve.tensor_copy(probT[:, g, :], bank[(g + 6) % 8][:, :]).then_inc(probT_dve, 1)
                for i in range(SPLITS - 1):
                    w_low(l, i)
                x_low(l)
                for i in range(SPLITS - 1, 2 * KC):
                    w_low(l, i)
                    if i in (KC + 2, KC + 4):
                        dve.wait_ge(chunk_used, 2 * KC * l + KC)
                        residual(l, (i - KC - 2) // 2, 0)
                for b in range(TB):
                    if b == 0:
                        dve.wait_ge(proj_pe, l + 1)
                    else:
                        dve.wait_ge(chunk_used, 2 * KC * (l + 1))
                    step(residual(l, b, 1))
                    norm_center(norm_variance(b, 2), h[:, b, :], b)
                scaled_columns(3 * l + 2, 2 * l + 1, [1])
                routing(l)
                dve.wait_ge(acc_init, TB * (l + 1))
                main, more = passes[l]
                with dve.Fori(0, ITERS) as it:
                    experts(l, main, 0, it)
                n = dve.value_load(fullest[0:1, l:l + 1], min_val=0, max_val=SEQ)
                with dve.If(n > SLOTS):
                    with dve.Fori(0, ROUNDS - 1) as rnd:
                        dve.tensor_scalar(slot[:, :, :, :], slot[:, :, :, :], -float(SLOTS), None, ALU.add)\
                           .then_inc(more.s["renumber"], 1)
                        with dve.Fori(0, ITERS) as it:
                            experts(l, more, rnd, it)
                if l < DEPTH - 1:
                    norm = [norm_stats(acc[:, b, :], b, D) for b in range(TB)]
                    for b in range(TB):
                        norm_center(norm[b], acc[:, b, :], b)
                else:
                    dve.wait_ge(par_in, 32 * (2 * l + 3))
                    layer_norms(lambda b: acc[:, b, :], lambda b: h[:, b, :], ln_par[:, 0, :], ln_par[:, 1, :], D,
                                result_ready)


_ORDER = ["x", "ln_in_g", "ln_in_b", "w_in", "w_out", "sg_ln_g", "sg_ln_b", "sg_w", "sg_b", "conv_w", "conv_b",
          "conv_ln_g", "conv_ln_b", "ln_mix_g", "ln_mix_b", "w_router", "router_bias", "w_gate", "w_up", "w_down",
          "ln_ffn_g", "ln_ffn_b"]


def kernel(**inputs):
    import concourse.bacc as bacc
    from concourse.bass_utils import run_bass_kernel_spmd

    nc = bacc.Bacc("TRN2", target_bir_lowering=False, num_devices=1)
    arrays, args = {}, []
    for name in _ORDER:
        a = np.ascontiguousarray(inputs[name])
        arrays[f"in_{name}"] = a
        args.append(nc.dram_tensor(f"in_{name}", a.shape, mybir.dt.from_np(a.dtype), kind="ExternalInput").ap())
    arrays["in_table"] = constants()
    args.append(nc.dram_tensor("in_table", (P, T_COLS), F32, kind="ExternalInput").ap())
    args.append(nc.dram_tensor("out_0", (1, SEQ, D), F32, kind="ExternalOutput").ap())
    trunk(nc, *args)
    r = run_bass_kernel_spmd(nc, [arrays], core_ids=[0])
    return r.results[0]["out_0"]
```
